# Optimizing a Trainium2 kernel written in Bass

```python
import math
import jax
import jax.numpy as jnp
from jax import lax
import numpy as np

D_MODEL = 1024
BATCH = 1
SEQ = 512
DEPTH = 2

N_MIXERS = 4
GROUP_WIDTH = D_MODEL // N_MIXERS
HEAD_DIM = 64
GROUP_HEADS = GROUP_WIDTH // HEAD_DIM
D_FF = 2816
SHORT_CONV = 4
CONF_KERNEL = 31
CONF_GROUPS = 4
GDN_CHUNK = 64
Q_BLOCK = 128
N_MEM = 256
MEM_HEADS = 4
MEM_HEAD_DIM = D_MODEL // MEM_HEADS
DN_ALPHA = float((2 * DEPTH) ** 0.25)
DN_INIT = float((8 * DEPTH) ** -0.25)
LN_EPS = 1e-5
RMS_EPS = 1e-6
L2_EPS = 1e-6
NEG_BIG = -1e30
IN_SPLITS = (3 * GROUP_WIDTH,
             GROUP_WIDTH,
             GROUP_HEADS,
             GROUP_HEADS,
             3 * GROUP_WIDTH,
             GROUP_HEADS,
             2 * GROUP_WIDTH,
             3 * GROUP_WIDTH)
IN_WIDTH = sum(IN_SPLITS)
IN_OFFSETS = tuple(int(o) for o in np.cumsum(IN_SPLITS)[:-1])

kernel_name = 'hybrid_headgroup_gdn_fox_conv_stickbreak'

def layer_norm(x, g, b):
    xf = x.astype(jnp.float32)
    mu = jnp.mean(xf, axis=-1, keepdims=True)
    var = jnp.mean(jnp.square(xf - mu), axis=-1, keepdims=True)
    y = (xf - mu) * lax.rsqrt(var + LN_EPS) * g.astype(jnp.float32) + b.astype(jnp.float32)
    return y.astype(x.dtype)

def swiglu(x, w_gate, w_up, w_down):
    return (jax.nn.silu(x @ w_gate) * (x @ w_up)) @ w_down

def causal_depthwise_conv(x, w):
    width, ch = w.shape
    xp = jnp.pad(x, ((0, 0), (width - 1, 0), (0, 0)))
    return lax.conv_general_dilated(xp, w[:, None, :].astype(x.dtype), window_strides=(1,), padding='VALID',
                                    dimension_numbers=('NWC', 'WIO', 'NWC'), feature_group_count=ch)

def to_heads(t):
    b, s, _ = t.shape
    return t.reshape(b, s, GROUP_HEADS, HEAD_DIM).transpose(0, 2, 1, 3)

def from_heads(t):
    b, h, s, d = t.shape
    return t.transpose(0, 2, 1, 3).reshape(b, s, h * d)

def l2_normalize(t):
    tf = t.astype(jnp.float32)
    return tf * lax.rsqrt(jnp.sum(tf * tf, axis=-1, keepdims=True) + L2_EPS)

def query_blocks(t):
    b, h, s = t.shape[:3]
    return jnp.moveaxis(t.reshape(b, h, s // Q_BLOCK, Q_BLOCK, *t.shape[3:]), 2, 0)

def merge_blocks(t):
    nb, b, h, qb, d = t.shape
    return jnp.moveaxis(t, 0, 2).reshape(b, h, nb * qb, d)

def gated_delta_rule_chunked(q, k, v, g, beta):
    f32 = jnp.float32
    b, h, s, dk = q.shape
    dv = v.shape[-1]
    c = GDN_CHUNK
    n = s // c
    q = q.astype(f32).reshape(b, h, n, c, dk) * (dk ** -0.5)
    k = k.astype(f32).reshape(b, h, n, c, dk)
    v = v.astype(f32).reshape(b, h, n, c, dv)
    beta = beta.astype(f32).reshape(b, h, n, c)
    g = jnp.cumsum(g.astype(f32).reshape(b, h, n, c), axis=-1)
    k_beta = k * beta[..., None]
    v_beta = v * beta[..., None]
    lower_incl = jnp.tril(jnp.ones((c, c), dtype=bool))
    strict_lower = jnp.tril(jnp.ones((c, c), dtype=bool), -1)
    decay = jnp.exp(jnp.where(lower_incl, g[..., :, None] - g[..., None, :], -jnp.inf))
    lkk = jnp.where(strict_lower, jnp.einsum('bhncd,bhnsd->bhncs', k_beta, k) * decay, 0.0)
    eye = jnp.eye(c, dtype=f32)
    t_inv = lax.linalg.triangular_solve(eye + lkk, jnp.broadcast_to(eye, lkk.shape), left_side=True, lower=True)
    u = jnp.einsum('bhncs,bhnsv->bhncv', t_inv, v_beta)
    w = jnp.einsum('bhncs,bhnsd->bhncd', t_inv, k_beta * jnp.exp(g)[..., None])
    a_qk = jnp.einsum('bhncd,bhnsd->bhncs', q, k) * decay
    g_last = g[..., -1]
    q_dec = q * jnp.exp(g)[..., None]
    k_dec = k * jnp.exp(g_last[..., None] - g)[..., None]

    def chunk_step(state, inp):
        q_c, k_c, u_c, w_c, a_c, gl_c = inp
        v_new = u_c - jnp.einsum('bhcd,bhdv->bhcv', w_c, state)
        o_c = jnp.einsum('bhcd,bhdv->bhcv', q_c, state) + jnp.einsum('bhcs,bhsv->bhcv', a_c, v_new)
        state = state * jnp.exp(gl_c)[..., None, None] + jnp.einsum('bhcd,bhcv->bhdv', k_c, v_new)
        return state, o_c

    xs = tuple(jnp.moveaxis(t, 2, 0) for t in (q_dec, k_dec, u, w, a_qk, g_last))
    state0 = jnp.zeros((b, h, dk, dv), f32)
    _, o = lax.scan(chunk_step, state0, xs)
    return jnp.moveaxis(o, 0, 2).reshape(b, h, s, dv)

def forgetting_attention(q, k, v, log_f):
    s_len, d = q.shape[2], q.shape[3]
    scale = d ** -0.5
    cum = jnp.cumsum(log_f.astype(jnp.float32), axis=-1)
    key_pos = jnp.arange(s_len)
    starts = jnp.arange(s_len // Q_BLOCK) * Q_BLOCK

    def block(args):
        q_blk, cum_blk, start = args
        logits = jnp.einsum('bhqd,bhkd->bhqk', q_blk, k).astype(jnp.float32) * scale
        logits = logits + cum_blk[..., :, None] - cum[..., None, :]
        causal = key_pos[None, :] <= (start + jnp.arange(Q_BLOCK))[:, None]
        probs = jax.nn.softmax(jnp.where(causal, logits, NEG_BIG), axis=-1)
        return jnp.einsum('bhqk,bhkd->bhqd', probs.astype(v.dtype), v)

    return merge_blocks(lax.map(block, (query_blocks(q), query_blocks(cum), starts)))

def stick_breaking_attention(q, k, v):
    s_len, d = q.shape[2], q.shape[3]
    scale = d ** -0.5
    key_pos = jnp.arange(s_len)
    starts = jnp.arange(s_len // Q_BLOCK) * Q_BLOCK

    def block(args):
        q_blk, start = args
        z = jnp.einsum('bhqd,bhkd->bhqk', q_blk, k).astype(jnp.float32) * scale
        strict = key_pos[None, :] < (start + jnp.arange(Q_BLOCK))[:, None]
        log_keep = jnp.where(strict, jax.nn.log_sigmoid(-z), 0.0)
        log_rest = lax.cumsum(log_keep, axis=3, reverse=True) - log_keep
        weights = jnp.where(strict, jnp.exp(jax.nn.log_sigmoid(z) + log_rest), 0.0)
        return jnp.einsum('bhqk,bhkd->bhqd', weights.astype(v.dtype), v)

    return merge_blocks(lax.map(block, (query_blocks(q), starts)))

def channel_group_norm(h, g, b):
    bsz, s, ch = h.shape
    hf = h.astype(jnp.float32).reshape(bsz, s, CONF_GROUPS, ch // CONF_GROUPS)
    mu = jnp.mean(hf, axis=-1, keepdims=True)
    var = jnp.mean(jnp.square(hf - mu), axis=-1, keepdims=True)
    hn = ((hf - mu) * lax.rsqrt(var + LN_EPS)).reshape(bsz, s, ch)
    return (hn * g.astype(jnp.float32) + b.astype(jnp.float32)).astype(h.dtype)

def parallel_head_group_mixers(x, w_in, gdn_conv_w, gdn_a_log, gdn_dt_bias, gdn_norm_g, fox_b_f,
                               conf_dw_w, conf_dw_b, conf_norm_g, conf_norm_b, w_out):
    f32 = jnp.float32
    proj = x @ w_in
    gdn_qkv, gdn_z, gdn_a, gdn_b, fox_qkv, fox_f, conf_glu, sb_qkv = jnp.split(proj, IN_OFFSETS, axis=-1)

    qkv = jax.nn.silu(causal_depthwise_conv(gdn_qkv, gdn_conv_w))
    q_a, k_a, v_a = (to_heads(t) for t in jnp.split(qkv, 3, axis=-1))
    beta = jax.nn.sigmoid(gdn_b.astype(f32)).transpose(0, 2, 1)
    log_decay = (-jnp.exp(gdn_a_log.astype(f32)) *
                 jax.nn.softplus(gdn_a.astype(f32) + gdn_dt_bias.astype(f32))).transpose(0, 2, 1)
    o_a = gated_delta_rule_chunked(l2_normalize(q_a), l2_normalize(k_a), v_a, log_decay, beta)
    o_a = o_a * lax.rsqrt(jnp.mean(o_a * o_a, axis=-1, keepdims=True) + RMS_EPS) * gdn_norm_g.astype(f32)
    y_a = (from_heads(o_a) * jax.nn.silu(gdn_z.astype(f32))).astype(x.dtype)

    q_b, k_b, v_b = (to_heads(t) for t in jnp.split(fox_qkv, 3, axis=-1))
    log_f = jax.nn.log_sigmoid(fox_f.astype(f32) + fox_b_f.astype(f32)).transpose(0, 2, 1)
    y_b = from_heads(forgetting_attention(q_b, k_b, v_b, log_f)).astype(x.dtype)

    val, gate = jnp.split(conf_glu, 2, axis=-1)
    c = causal_depthwise_conv(val * jax.nn.sigmoid(gate), conf_dw_w) + conf_dw_b
    y_c = jax.nn.silu(channel_group_norm(c, conf_norm_g, conf_norm_b)).astype(x.dtype)

    q_d, k_d, v_d = (to_heads(t) for t in jnp.split(sb_qkv, 3, axis=-1))
    y_d = from_heads(stick_breaking_attention(q_d, k_d, v_d)).astype(x.dtype)

    return jnp.concatenate([y_a, y_b, y_c, y_d], axis=-1) @ w_out

def memory_cross_attention(x, mem, w_q, w_kv, w_o):
    b, s, _ = x.shape
    m = mem.shape[1]
    q = (x @ w_q).reshape(b, s, MEM_HEADS, MEM_HEAD_DIM)
    k, v = jnp.split(mem @ w_kv, 2, axis=-1)
    k = k.reshape(b, m, MEM_HEADS, MEM_HEAD_DIM)
    v = v.reshape(b, m, MEM_HEADS, MEM_HEAD_DIM)
    scores = jnp.einsum('bthd,bmhd->bhtm', q, k).astype(jnp.float32) * (MEM_HEAD_DIM ** -0.5)
    probs = jax.nn.softmax(scores, axis=-1).astype(v.dtype)
    out = jnp.einsum('bhtm,bmhd->bthd', probs, v).reshape(b, s, D_MODEL)
    return out @ w_o

def setup_inputs(seed: int = 0) -> dict:
    key = jax.random.key(seed)
    keys = iter(jax.random.split(key, 40))
    f32 = jnp.float32
    L = DEPTH

    def normal(shape, scale):
        return jax.random.normal(next(keys), shape, f32) * scale

    def gain(shape):
        return 1.0 + normal(shape, 0.02)

    dt = jnp.exp(jax.random.uniform(next(keys), (L, GROUP_HEADS), f32, math.log(1e-3), math.log(1e-1)))
    gdn_dt_bias = dt + jnp.log(-jnp.expm1(-dt))
    gdn_a_log = jnp.log(jax.random.uniform(next(keys), (L, GROUP_HEADS), f32, 1.0, 16.0))
    d_in = D_MODEL ** -0.5
    return {
        'x': normal((BATCH, SEQ, D_MODEL), 1.0),
        'mem': normal((BATCH, N_MEM, D_MODEL), 1.0),
        'ffn1_w_gate': normal((L, D_MODEL, D_FF), d_in),
        'ffn1_w_up': normal((L, D_MODEL, D_FF), d_in),
        'ffn1_w_down': normal((L, D_FF, D_MODEL), DN_INIT * D_FF ** -0.5),
        'ln_ffn1_g': gain((L, D_MODEL)),
        'ln_ffn1_b': normal((L, D_MODEL), 0.02),
        'w_in': normal((L, D_MODEL, IN_WIDTH), d_in),
        'gdn_conv_w': normal((L, SHORT_CONV, 3 * GROUP_WIDTH), SHORT_CONV ** -0.5),
        'gdn_a_log': gdn_a_log,
        'gdn_dt_bias': gdn_dt_bias,
        'gdn_norm_g': gain((L, HEAD_DIM)),
        'fox_b_f': 3.0 + normal((L, GROUP_HEADS), 0.1),
        'conf_dw_w': normal((L, CONF_KERNEL, GROUP_WIDTH), CONF_KERNEL ** -0.5),
        'conf_dw_b': normal((L, GROUP_WIDTH), 0.02),
        'conf_norm_g': gain((L, GROUP_WIDTH)),
        'conf_norm_b': normal((L, GROUP_WIDTH), 0.02),
        'w_out': normal((L, D_MODEL, D_MODEL), DN_INIT * d_in),
        'ln_mix_g': gain((L, D_MODEL)),
        'ln_mix_b': normal((L, D_MODEL), 0.02),
        'mem_w_q': normal((L, D_MODEL, D_MODEL), d_in),
        'mem_w_kv': normal((L, D_MODEL, 2 * D_MODEL), d_in),
        'mem_w_o': normal((L, D_MODEL, D_MODEL), DN_INIT * d_in),
        'ln_mem_g': gain((L, D_MODEL)),
        'ln_mem_b': normal((L, D_MODEL), 0.02),
        'ffn2_w_gate': normal((L, D_MODEL, D_FF), d_in),
        'ffn2_w_up': normal((L, D_MODEL, D_FF), d_in),
        'ffn2_w_down': normal((L, D_FF, D_MODEL), DN_INIT * D_FF ** -0.5),
        'ln_ffn2_g': gain((L, D_MODEL)),
        'ln_ffn2_b': normal((L, D_MODEL), 0.02),
    }

def reference(x, mem, ffn1_w_gate, ffn1_w_up, ffn1_w_down, ln_ffn1_g, ln_ffn1_b,
              w_in, gdn_conv_w, gdn_a_log, gdn_dt_bias, gdn_norm_g, fox_b_f,
              conf_dw_w, conf_dw_b, conf_norm_g, conf_norm_b, w_out, ln_mix_g, ln_mix_b,
              mem_w_q, mem_w_kv, mem_w_o, ln_mem_g, ln_mem_b,
              ffn2_w_gate, ffn2_w_up, ffn2_w_down, ln_ffn2_g, ln_ffn2_b):
    for i in range(DEPTH):
        x = layer_norm(DN_ALPHA * x + 0.5 * swiglu(x, ffn1_w_gate[i], ffn1_w_up[i], ffn1_w_down[i]),
                       ln_ffn1_g[i], ln_ffn1_b[i])
        mix = parallel_head_group_mixers(x, w_in[i], gdn_conv_w[i], gdn_a_log[i], gdn_dt_bias[i], gdn_norm_g[i],
                                         fox_b_f[i], conf_dw_w[i], conf_dw_b[i], conf_norm_g[i], conf_norm_b[i],
                                         w_out[i])
        x = layer_norm(DN_ALPHA * x + mix, ln_mix_g[i], ln_mix_b[i])
        x = layer_norm(DN_ALPHA * x + memory_cross_attention(x, mem, mem_w_q[i], mem_w_kv[i], mem_w_o[i]),
                       ln_mem_g[i], ln_mem_b[i])
        x = layer_norm(DN_ALPHA * x + 0.5 * swiglu(x, ffn2_w_gate[i], ffn2_w_up[i], ffn2_w_down[i]),
                       ln_ffn2_g[i], ln_ffn2_b[i])
    return x


_drawn_inputs = setup_inputs


def setup_inputs(seed=0):
    import zlib

    import numpy as np

    out = dict(_drawn_inputs(seed))
    spreads = {}
    factors = {'gdn_norm_g': 25.386,
     'fox_b_f': 64.0,
     'conf_dw_b': 8.0,
     'conf_norm_g': 22.235,
     'conf_norm_b': 21.691}
    for name, (base, spread) in spreads.items():
        noise = np.random.default_rng([zlib.crc32(name.encode()), seed]).standard_normal(out[name].shape)
        drawn = base * np.exp(spread * noise) if base else spread * noise
        out[name] = jnp.asarray(drawn.astype(out[name].dtype))
    for name, factor in factors.items():
        out[name] = (out[name] * factor).astype(out[name].dtype)
    return out
```

```python
import numpy as np
import concourse.bass as bass
from concourse import mybir

P = 128
D, SEQ, DEPTH, FF, NMEM = 1024, 512, 2, 2816, 256
KT = D // P
TT = SEQ // P
FT = FF // P
H, HD = 4, 64
MH = 4
NC = SEQ // 64
ALPHA = float((2 * DEPTH) ** 0.25)
LN_EPS, RMS_EPS, L2_EPS = 1e-5, 1e-6, 1e-6
KCONV, KDW = 4, 31
BW, DW_W = KT * P, (FT // 2) * P

B_UP1 = 0
B_DN1 = B_UP1 + 2 * FT
B_IN = B_DN1 + 16
B_V = B_IN + 20
B_OUT = B_V + 4
B_MK = B_OUT + 8
B_MV = B_MK + 8
B_MQ = B_MV + 8
B_MO = B_MQ + 8
B_UP2 = B_MO + 8
B_DN2 = B_UP2 + 2 * FT
B_END = B_DN2 + 16

F32 = mybir.dt.float32
F32R = mybir.dt.float32r
ALU = mybir.AluOpType
ACT = mybir.ActivationFunctionType
AX = mybir.AxisListType

CNAMES = ["ident", "uall", "ublk", "blk", "nlt", "none", "ones",
          "negst", "neginc", "mdt", "ml", "mst", "lv0", "lv1", "lv2", "lv3", "lv4", "lv5"]
NCST = len(CNAMES) * P
P_LN, P_GCONV, P_DWW, P_DWB, P_CNG, P_CNB, P_GNG, P_DT, P_ALOG, P_FB, P_GW = (
    0, 64, 88, 150, 152, 154, 156, 157, 161, 165, 169)
NPRM = P_GW + KT * 12


def constants():
    i = np.arange(P)
    r, c = np.broadcast_arrays(i[:, None], i[None, :])
    blk = (r // 64) == (c // 64)
    z = {
        "ident": r == c, "uall": r <= c, "ublk": blk & (r <= c), "blk": blk,
        "nlt": -1.0 * (r >= c), "none": -1.0 * (r >= 0), "ones": r >= 0,
        "negst": -1e30 * (r >= c), "neginc": -1e30 * (c > r),
        "mdt": blk & (r <= c), "ml": blk & (c < r), "mst": r < c,
    }
    for k in range(6):
        s = 1 << k
        z[f"lv{k}"] = (r // (2 * s) == c // (2 * s)) & (r % (2 * s) >= s) & (c % (2 * s) < s)
    return np.concatenate([z[n].astype(np.float32) for n in CNAMES], axis=1)


def need(eng, sem, value):
    if not isinstance(value, int) or value > 0:
        eng.wait_ge(sem, value)


def run_blocks(eng, c0, n, body):
    full = n // 4
    if full > 1:
        with eng.Fori(0, full) as g:
            for j in range(4):
                body(g, c0 + j)
    else:
        for j in range(4 * full):
            body(0, c0 + j)
    for j in range(n - 4 * full):
        body(0, c0 + 4 * full + j)


def build_program(nc, xt_in, memt_in, wst, wdn, prm_in, cst_in, out):
    sb = nc.alloc_sbuf_tensor
    XT = sb("x_t", [P, KT, SEQ], F32)
    XH = sb("x_hi", [P, KT, SEQ], F32R)
    XL = sb("x_lo", [P, KT, SEQ], F32R)
    RAW = sb("w_raw", [P, 4, DW_W], F32)
    WH = sb("w_hi", [P, 2, DW_W], F32R)
    WL = sb("w_lo", [P, 2, DW_W], F32R)
    CST = sb("consts", [P, NCST], F32)
    PRM = sb("params", [P, NPRM], F32)
    T = sb("scratch", [P, 6, SEQ], F32)
    SM = sb("small", [P, 560], F32)
    a0 = (nc.sbuf_base + 31) // 32 * 32
    n_arena = min((nc.sbuf_usable_end - a0) // 4 - 8, 23560)
    sb("arena", [P, n_arena], F32)

    def at(name, col, shape, dt=F32):
        size = 1
        for s in shape:
            size *= s
        assert col + size <= n_arena, (name, col + size, n_arena)
        return nc.alloc_sbuf_tensor_at(name, [P] + shape, dt, offset=a0 + 4 * col)

    HH = at("h_hi", 0, [FT, SEQ], F32R)
    HL = at("h_lo", FT * SEQ, [FT, SEQ], F32R)
    RAW6 = at("gdn_raw", 0, [6, SEQ + 3])
    GLU = at("glu", 3096, [2, SEQ + 30])
    C6 = at("gdn_qkv", 4184, [6, SEQ])
    DWA = at("dw_acc", 7256, [2, SEQ])
    ZS = at("silu_z", 8280, [2, SEQ])
    FQ = at("fox_q", 9304, [2, SEQ])
    FK = at("fox_k", 10328, [2, SEQ])
    SQ = at("sb_q", 11352, [2, SEQ])
    SK = at("sb_k", 12376, [2, SEQ])
    V = at("v_tok", 13400, [TT, 512])
    CUMB = at("fox_cum", 15448, [H, SEQ])
    VB = at("v_beta", 17496, [TT * H, HD])
    KBE = at("k_beta_exp", 18520, [TT * H, HD])
    KD = at("k_decayed", 19544, [TT * H, HD])
    SP = at("softplus", 20568, [2, 1280])
    SW = at("sb_weights", 0, [2, 1280])
    PT = at("fox_p_t", 20568, [2, SEQ])
    L = at("gdn_l", 9304, [H, SEQ])
    X = at("gdn_x", 11352, [H, SEQ])
    Y = at("gdn_y", 13400, [H, SEQ])
    AT = at("gdn_a_t", 15448, [H, SEQ])
    NB = at("gdn_n", 20568, [H, SEQ])
    QB = at("gdn_q", 0, [H, SEQ])
    U = at("gdn_u", 2056, [TT * H, HD])
    WT = at("gdn_w_t", 3096, [2, SEQ])
    OT = at("gdn_o", 9304, [TT * H, HD])
    VN = at("gdn_v_new", 10328, [H, HD])
    OSQ = at("gdn_o_squared", 11352, [TT * H, HD])
    MT = at("mem_t", 0, [KT, NMEM])
    MTH = at("mem_hi", 2048, [KT, NMEM], F32R)
    MTL = at("mem_lo", 4096, [KT, NMEM], F32R)
    KM = at("mem_k", 6144, [KT, NMEM])
    VM = at("mem_v", 8192, [2, D])
    MQ = at("mem_q", 10240, [KT, SEQ])
    MP = at("mem_p_t", 14336, [2, 2, SEQ])

    def small(c, n):
        return SM[:, c:c + n]

    G, U8, AB = small(0, 48), small(48, 32), small(80, 32)
    EA, EB, SPL = small(112, 4), small(116, 16), small(132, 32)
    LD, LF, BETA = small(164, 16), small(180, 16), small(196, 16)
    CUM48, EG, KDC = small(212, 48), small(260, 16), small(276, 16)
    BEG, EG8, EGL = small(292, 16), small(308, 16), small(324, 16)
    NM, RS, RI = small(340, 16), small(356, 16), small(372, 16)
    OS16, EPS = small(388, 16), small(404, 4)
    ST = SM[:, 412:540].rearrange("p (a b) -> p a b", a=2)
    TMP16 = small(540, 16)

    ps = [nc.alloc_psum_tensor(f"bank{i}", [P, 512], F32) for i in range(8)]

    def cst(n, rows=P):
        k = CNAMES.index(n)
        return CST[:, k * P:(k + 1) * P]

    def prm(c, n=1):
        return PRM[:, c:c + n]

    def f32(ap):
        return ap.bitcast(F32)

    load_sem, prep = nc.alloc_semaphore("inputs_landed"), nc.alloc_semaphore("x_split")
    sems = {}

    def S(name):
        if name not in sems:
            sems[name] = nc.alloc_semaphore(name)
        return sems[name]

    per_use = {"y": KT, "ysum": KT - 1, "sq": KT, "qsum": KT - 1, "stats": 1, "ln": 5, "cen": KT, "sd": 1,
               "norm": KT, "aff": KT, "xhi": KT, "xlo": KT, "silu": FT, "h": FT, "hh": FT, "hl": FT}

    def base(tag, name):
        return per_use[name] * (("ad" if per_use[name] == FT else "abcd").index(tag))

    def after(eng, tag, name, value):
        if not isinstance(value, int) or value > 0:
            eng.wait_ge(S("each_" + name), base(tag, name) + value)

    landed = [S(f"landed{r}") for r in range(4)]
    hi_done, split_done, used = S("hi_done"), S("split_done"), S("blocks_used")

    def width(c):
        return DW_W if B_DN1 <= c < B_IN or B_DN2 <= c < B_END else BW

    def load_block(sp, li, g, c):
        need(sp, split_done, 4 * g + c - 3)
        if B_DN1 <= c < B_IN:
            src = wdn[li, 4 * g + (c - B_DN1)]
        elif c >= B_DN2:
            src = wdn[li, 4 * g + (c - B_DN2 + 16)]
        else:
            src = wst[li, 4 * g + (c if c < B_DN1 else c - 16)]
        sp.dma_start(RAW[:, c % 4, :width(c)], src).then_inc(landed[c % 4], 16)

    def split_hi(act, g, c):
        act.wait_ge(landed[c % 4], 16 * g + 16 * (c // 4 + 1))
        need(act, used, 4 * g + c - 1)
        act.activation(WH[:, c % 2, :width(c)], RAW[:, c % 4, :width(c)], ACT.Copy).then_inc(hi_done, 1)

    def split_lo(pool, g, c):
        pool.wait_ge(hi_done, 4 * g + c + 1)
        pool.tensor_tensor(WL[:, c % 2, :width(c)], RAW[:, c % 4, :width(c)],
                           f32(WH[:, c % 2, :width(c)]), ALU.subtract).then_inc(split_done, 1)

    def mm3(pe, o, lh, ll, rh, rl, start, stop):
        pe.matmul(o, lh, rh, start=start, stop=False)
        pe.matmul(o, lh, rl, start=False, stop=False)
        return pe.matmul(o, ll, rh, start=False, stop=stop)

    def pe_block(pe, g, c, bank, rh, rl, k0=0, n=KT, total=KT, cols=SEQ, ready=None):
        pe.wait_ge(split_done, 4 * g + c + 1)
        for i in range(n):
            k = k0 + i
            if ready is not None:
                after(pe, *ready, k + 1)
            w = slice(i * P, (i + 1) * P)
            last = mm3(pe, bank[:, :cols], WH[:, c % 2, w], WL[:, c % 2, w], rh[:, k, :], rl[:, k, :],
                       k == 0, k == total - 1)
        last.then_inc(used, 1)

    def ln_gather_dve(dve, tag, scale, ready):
        for d in range(KT):
            dve.wait_ge(used, ready(d))
            dve.scalar_tensor_tensor(XT[:, d], XT[:, d], scale, ps[4 + d % 2][:], ALU.mult,
                                     ALU.add).then_inc(S("each_y"), 1)
            dve.wait_ge(S("each_y"), base(tag, "y") + d + 1)
            if d >= 1:
                after(dve, tag, "ysum", d - 1)
                dve.tensor_tensor(T[:, 0], XT[:, 0] if d == 1 else T[:, 0], XT[:, d],
                                  ALU.add).then_inc(S("each_ysum"), 1)
                dve.wait_ge(S("each_sq"), base(tag, "sq") + d + 1)
                after(dve, tag, "qsum", d - 1)
                dve.tensor_tensor(T[:, 1], T[:, 2] if d == 1 else T[:, 1], T[:, 2 + d % 2],
                                  ALU.add).then_inc(S("each_qsum"), 1)

    def ln_square_act(act, tag, d):
        act.wait_ge(S("each_y"), base(tag, "y") + d + 1)
        if d >= 2:
            act.wait_ge(S("each_qsum"), base(tag, "qsum") + max(1, d - 2))
        act.activation(T[:, 2 + d % 2], XT[:, d], ACT.Square).then_inc(S("each_sq"), 1)

    def ln_stats_pe(pe, tag):
        pe.wait_ge(S("each_ysum"), base(tag, "ysum") + KT - 1)
        pe.matmul(ps[6][:], cst("ones"), T[:, 0], start=True, stop=True)
        pe.wait_ge(S("each_qsum"), base(tag, "qsum") + KT - 1)
        pe.matmul(ps[7][:], cst("ones"), T[:, 1], start=True, stop=True).then_inc(S("each_stats"), 1)

    def ln_dve(dve, tag, eps):
        st, s0 = S("each_ln"), base(tag, "ln")
        dve.wait_ge(S("each_stats"), base(tag, "stats") + 1)
        dve.tensor_scalar(T[:, 4], ps[6][:], 1.0 / D, None, ALU.mult).then_inc(st, 1)
        dve.wait_ge(st, s0 + 1)
        dve.tensor_tensor(T[:, 5], T[:, 4], T[:, 4], ALU.mult).then_inc(st, 1)
        dve.wait_ge(st, s0 + 2)
        dve.scalar_tensor_tensor(T[:, 2], ps[7][:], 1.0 / D, T[:, 5], ALU.mult, ALU.subtract).then_inc(st, 1)
        dve.wait_ge(st, s0 + 3)
        dve.tensor_scalar(T[:, 2], T[:, 2], 0.0, eps, ALU.max, ALU.add).then_inc(st, 1)
        for d in range(KT):
            ins = dve.tensor_tensor(XT[:, d], XT[:, d], T[:, 4], ALU.subtract)
            ins.then_inc(S("each_cen"), 1)
        dve.wait_ge(S("each_sd"), base(tag, "sd") + 1)
        dve.reciprocal(T[:, 3], T[:, 2]).then_inc(st, 1)
        dve.wait_ge(st, s0 + 5)
        for d in range(KT):
            dve.wait_ge(S("each_cen"), base(tag, "cen") + d + 1)
            dve.tensor_tensor(XT[:, d], XT[:, d], T[:, 3], ALU.mult).then_inc(S("each_norm"), 1)

    def ln_sqrt_act(act, tag):
        act.wait_ge(S("each_ln"), base(tag, "ln") + 4)
        act.activation(T[:, 2], T[:, 2], ACT.Sqrt).then_inc(S("each_sd"), 1)

    def ln_affine_act(act, tag, n, d):
        if d < KT:
            act.wait_ge(S("each_norm"), base(tag, "norm") + d + 1)
            act.activation(XT[:, d], XT[:, d], ACT.Identity, bias=prm(P_LN + 16 * n + 8 + d),
                           scale=prm(P_LN + 16 * n + d)).then_inc(S("each_aff"), 1)
        if d >= 1:
            act.wait_ge(S("each_aff"), base(tag, "aff") + d)
            act.activation(XH[:, d - 1], XT[:, d - 1], ACT.Copy).then_inc(S("each_xhi"), 1)

    def ln_lo_pool(pool, tag, d):
        pool.wait_ge(S("each_xhi"), base(tag, "xhi") + d + 1)
        pool.tensor_tensor(XL[:, d], XT[:, d], f32(XH[:, d]), ALU.subtract).then_inc(S("each_xlo"), 1)

    def ffn_pe(pe, tag, b0, ready):
        up, dn = b0, b0 + 2 * FT

        def pair(g, first):
            for j in range(2):
                f = 2 * g + j
                if not first:
                    pe.wait_ge(S("each_silu"), base(tag, "silu") + f - 1)
                pe_block(pe, g, up + 2 * j, ps[j], XH, XL, ready=ready if first and j == 0 else None)
                if not first:
                    pe.wait_ge(S("each_h"), base(tag, "h") + f - 1)
                pe_block(pe, g, up + 2 * j + 1, ps[2 + j], XH, XL)

        pair(0, True)
        with pe.Fori(1, FT // 2) as g:
            pair(g, False)

        def down(g, first):
            for j in range(2):
                d = 2 * g + j
                if not first:
                    pe.wait_ge(S("each_y"), base(tag, "y") + d - 1)
                for half in range(2):
                    pe_block(pe, g, dn + 2 * j + half, ps[4 + j], HH, HL, k0=half * (FT // 2), n=FT // 2,
                             total=FT, ready=(tag, "hl") if first and j == 0 else None)

        down(0, True)
        with pe.Fori(1, KT // 2) as g:
            down(g, False)
        ln_stats_pe(pe, tag)

    def ffn_act(act, tag, b0, nxt):
        up, dn = b0, b0 + 2 * FT
        for c in (up, up + 1):
            if c < 2:
                split_hi(act, 0, c)

        def pair(g, first):
            for j in range(2):
                f = 2 * g + j
                c = up + 2 * j
                split_hi(act, g, c + 2) if not isinstance(g, int) else split_hi(act, 0, 4 * g + c + 2)
                act.wait_ge(used, 4 * g + c + 1)
                if not first:
                    act.wait_ge(S("each_h"), base(tag, "h") + f - 1)
                act.activation(T[:, j], ps[j][:], ACT.Silu).then_inc(S("each_silu"), 1)
                split_hi(act, g, c + 3) if not isinstance(g, int) else split_hi(act, 0, 4 * g + c + 3)

        pair(0, True)
        with act.Fori(1, FT // 2 - 1) as g:
            pair(g, False)
        pair(FT // 2 - 1, False)
        for d in range(KT):
            for c in (dn + 2 * d + 2, dn + 2 * d + 3):
                if c < nxt:
                    split_hi(act, 0, c)
            ln_square_act(act, tag, d)

    def ffn_dve(dve, tag, b0):
        def pair(g, first):
            for j in range(2):
                f = 2 * g + j
                dve.wait_ge(S("each_silu"), base(tag, "silu") + f + 1)
                dve.wait_ge(used, 4 * g + b0 + 2 * j + 2)
                if not first:
                    dve.wait_ge(S("each_hl"), base(tag, "hl") + f - 1)
                dve.tensor_tensor(T[:, 2 + j], T[:, j], ps[2 + j][:], ALU.mult).then_inc(S("each_h"), 1)
                dve.wait_ge(S("each_h"), base(tag, "h") + f + 1)
                dve.tensor_copy(HH[:, f], T[:, 2 + j]).then_inc(S("each_hh"), 1)
                dve.wait_ge(S("each_hh"), base(tag, "hh") + f + 1)
                dve.tensor_tensor(HL[:, f], T[:, 2 + j], f32(HH[:, f]), ALU.subtract).then_inc(S("each_hl"), 1)

        pair(0, True)
        with dve.Fori(1, FT // 2) as g:
            pair(g, False)
        dn = b0 + 2 * FT
        ln_gather_dve(dve, tag, 2.0 * ALPHA, lambda d: dn + 2 * d + 2)
        ln_dve(dve, tag, 4.0 * LN_EPS)

    def half(h):
        return slice(64 * (h % 2), 64 * (h % 2) + 64)

    SBB = [(0, 0, 512), (1, 0, 384), (2, 0, 256), (1, 384, 128)]
    SBO = [0, 512, 1024, 896]
    SBW = [(0, 512), (512, 512), (1024, 256)]

    def evac_wait(eng, i):
        eng.wait_ge(S(f"proj_evac{i % 4}"), i // 4 + 1)

    with nc.Block() as block:
        @block.sync
        def _(sp):
            sp.dma_start(XT[:], xt_in).then_inc(load_sem, 16)
            sp.dma_start(CST[:], cst_in).then_inc(load_sem, 16)
            sp.wait_ge(load_sem, 32)

        @block.vector
        def _(dve):
            for i, v in enumerate((L2_EPS, LN_EPS, RMS_EPS, 0.0)):
                dve.memset(EPS[:, i:i + 1], v)
            dve.wait_ge(load_sem, 32)
            dve.tensor_copy(XH[:], XT[:]).then_inc(prep, 1)
            dve.wait_ge(prep, 1)
            dve.tensor_tensor(XL[:], XT[:], f32(XH[:]), ALU.subtract).then_inc(prep, 1)
            dve.wait_ge(prep, 2)

    with nc.Fori(0, DEPTH) as li:
        with nc.Block() as block:
            @block.sync
            def _(sp):
                sp.dma_start(PRM[:], prm_in[li]).then_inc(S("prm_landed"), 16)
                for c in range(4):
                    load_block(sp, li, 0, c)
                run_blocks(sp, 4, B_DN1 - 4, lambda g, c: load_block(sp, li, g, c))
                run_blocks(sp, B_DN1, 16, lambda g, c: load_block(sp, li, g, c))
                run_blocks(sp, B_IN, B_OUT + 4 - B_IN, lambda g, c: load_block(sp, li, g, c))
                sp.wait_ge(used, B_OUT + 1)
                sp.dma_start(MT[:], memt_in).then_inc(S("mem_landed"), 16)
                run_blocks(sp, B_OUT + 4, B_DN2 - B_OUT - 4, lambda g, c: load_block(sp, li, g, c))
                run_blocks(sp, B_DN2, 16, lambda g, c: load_block(sp, li, g, c))

            @block.gpsimd
            def _(pool):
                def lo(c0, c1):
                    run_blocks(pool, c0, c1 - c0, lambda g, c: split_lo(pool, g, c))

                lo(0, B_DN1)
                lo(B_DN1, B_IN)
                lo(B_IN, B_IN + 2)
                for d in range(KT):
                    ln_lo_pool(pool, "a", d)
                lo(B_IN + 2, B_OUT + 2)
                for j in range(2):
                    pool.wait_ge(S("yc_hi"), j + 1)
                    pool.tensor_tensor(XL[:, 4 + j], T[:, j], f32(XH[:, 4 + j]), ALU.subtract).then_inc(S("yc_lo"), 1)
                for i in range(6 * H):
                    k, h = i // H, i % H
                    pool.wait_ge(S("gdn_l"), h + 1)
                    if i >= H:
                        if k == 1:
                            pool.wait_ge(S("gdn_t0"), h + 1)
                            pool.wait_ge(S("gdn_xy"), h + 1)
                        else:
                            pool.wait_ge(S("gdn_q"), i - 2 * H + 1)
                    pool.tensor_tensor(
                        NB[:, h].rearrange("p (t c) -> p t c", t=TT), L[:, h].rearrange("p (t c) -> p t c", t=TT),
                        cst(f"lv{k}").unsqueeze(1).to_broadcast([P, TT, P]), ALU.mult).then_inc(S("gdn_nb"), 1)
                for j in range(2):
                    pool.wait_ge(S("ya_hi"), j + 1)
                    pool.tensor_tensor(XL[:, j], T[:, j], f32(XH[:, j]), ALU.subtract).then_inc(S("ya_lo"), 1)
                lo(B_OUT + 2, B_MK + 2)
                pool.wait_ge(S("mem_hi"), 1)
                pool.tensor_tensor(MTL[:], MT[:], f32(MTH[:]), ALU.subtract).then_inc(S("mem_lo"), 1)
                for i in range(16):
                    split_lo(pool, 0, B_MK + 2 + i)
                    if 4 <= i < 12:
                        ln_lo_pool(pool, "b", i - 4)
                lo(B_MQ + 2, B_MO + 2)
                lo(B_MO + 2, B_UP2 + 2)
                for d in range(KT):
                    ln_lo_pool(pool, "c", d)
                lo(B_UP2 + 2, B_DN2)
                lo(B_DN2, B_END)
                for d in range(KT):
                    ln_lo_pool(pool, "d", d)

            @block.tensor
            def _(pe):
                ffn_pe(pe, "a", B_UP1, None)

                after(pe, "a", "aff", KT)
                for t in range(TT):
                    for k in range(KT):
                        last = pe.matmul(ps[4][:, 12 * t:12 * t + 12], XT[:, k, t * P:(t + 1) * P],
                                         PRM[:, P_GW + 12 * k:P_GW + 12 * k + 12], start=k == 0, stop=k == KT - 1)
                last.then_inc(S("gates"), 1)

                for i in range(20):
                    if i >= 4:
                        evac_wait(pe, i - 4)
                    pe_block(pe, 0, B_IN + i, ps[i % 4], XH, XL, ready=("a", "xlo") if i == 0 else None)
                    if i == 6:
                        pe.wait_ge(S("gates_log"), 1)
                        pe.matmul(ps[5][:, 0:16], cst("ublk"), LD, start=True, stop=True)
                        pe.matmul(ps[5][:, 16:32], cst("blk"), LD, start=True, stop=True)
                        for h in range(H):
                            for t in range(TT):
                                c = 32 + 8 * (h // 2) + 2 * t
                                last = pe.matmul(ps[5][half(h), c:c + 2],
                                                 LD[:, 4 * t + h:4 * t + h + 1].to_broadcast([P, 64]),
                                                 cst("blk")[:, 0:P:64], start=True, stop=True)
                        last.then_inc(S("decays"), 1)
                    if i == 15:
                        pe.wait_ge(S("gates_evac"), 1)
                        pe.wait_ge(S("decays_evac"), 1)
                        for t in range(4):
                            pe.wait_ge(S("qk_sq"), t + 1)
                            pe.matmul(ps[4 + t][:], cst("blk"), T[:, 2 + t], start=True,
                                      stop=True).then_inc(S("qk_sum"), 1)
                pe.wait_ge(S("qk_root"), 4)
                for i in range(4):
                    c = B_V + i
                    pe.wait_ge(split_done, c + 1)
                    for kk in range(2):
                        k = 2 * i + kk
                        w = slice(512 * kk, 512 * kk + 512)
                        for t in range(TT):
                            tok = slice(t * P, (t + 1) * P)
                            pe.matmul(ps[4 + t][:], XH[:, k, tok], WH[:, c % 2, w], start=k == 0, stop=False)
                            pe.matmul(ps[4 + t][:], XH[:, k, tok], WL[:, c % 2, w], start=False, stop=False)
                            last = pe.matmul(ps[4 + t][:], XL[:, k, tok], WH[:, c % 2, w], start=False,
                                             stop=k == KT - 1)
                    last.then_inc(used, 1)

                for i in range(16, 20):
                    evac_wait(pe, i)
                for q in range(2):
                    pe.wait_ge(S("qk_norm"), 3 + q)
                    for t in range(TT):
                        last = pe.transpose(ps[q][:, t * P:(t + 1) * P], C6[:, 2 + q, t * P:(t + 1) * P], cst("ident"))
                    last.then_inc(S("kv_tok"), 1)
                pe.wait_ge(S("qkv_silu"), 6)
                for q in range(2):
                    for t in range(TT):
                        last = pe.transpose(ps[2 + q][:, t * P:(t + 1) * P], C6[:, 4 + q, t * P:(t + 1) * P],
                                            cst("ident"))
                    last.then_inc(S("kv_tok"), 1)
                pe.wait_ge(S("kv_scaled"), 6)
                pe.wait_ge(S("dw"), 2 * KDW)
                for j in range(2):
                    pe.matmul(ps[2 * j][:], cst("blk"), DWA[:, j], start=True, stop=True)
                    pe.wait_ge(S("dw_sq"), j + 1)
                    pe.matmul(ps[2 * j + 1][:], cst("blk"), T[:, 4 + j], start=True, stop=True).then_inc(S("dw_sum"), 1)

                pe.wait_ge(S("conv_norm"), 4)
                pe.wait_ge(S("v_evac"), TT)

                def sb_scores(h):
                    r, q = half(h), h // 2
                    need(pe, S("sb_w"), 3 * (h - 1))
                    for sblk in (0, 1, 3, 2):
                        bank, c0, w = SBB[sblk]
                        last = pe.matmul(ps[3 * (h % 2) + bank][:, c0:c0 + w], SK[r, q, sblk * P:(sblk + 1) * P],
                                         SQ[r, q, sblk * P:], start=c0 == 0, stop=True, skip_group_check=True)
                        if sblk != 1:
                            last.then_inc(S("sb_z"), 1)

                def sb_sums(h):
                    pe.wait_ge(S("sb_mask"), 3 * h + 3)
                    for sblk in (0, 1, 3, 2):
                        bank, c0, w = SBB[sblk]
                        o = ps[3 * (h % 2) + bank]
                        for j in range(sblk, 4):
                            pe.matmul(o[:, c0 + (j - sblk) * P:c0 + w], cst("nlt" if j == sblk else "none"),
                                      SP[:, h % 2, SBO[j]:SBO[j] + SEQ - j * P], start=False, stop=False,
                                      skip_group_check=True)
                        last = pe.matmul(o[:, c0:c0 + P], cst("ident"), cst("negst"), start=False, stop=True,
                                         skip_group_check=True)
                        if sblk != 1:
                            last.then_inc(S("sb_sum"), 1)

                def sb_values(h):
                    pe.wait_ge(S("sb_w"), 3 * h + 3)
                    for s in range(4):
                        last = pe.matmul(ps[6 + h // 2][half(h), s * P:], V[:, s, 256 + 64 * h:256 + 64 * h + 64],
                                         SW[:, h % 2, SBO[s]:SBO[s] + SEQ - s * P], start=s == 0, stop=s == 3,
                                         skip_group_check=True)
                    last.then_inc(S("sb_o"), 1)

                sb_scores(0)
                sb_scores(1)
                for h in range(H):
                    sb_sums(h)
                    if h + 2 < H:
                        sb_scores(h + 2)
                    sb_values(h)

                pe.wait_ge(S("sb_w"), 12)
                for h in range(H):
                    for t in range(TT):
                        for j in range(t + 1):
                            last = pe.matmul(ps[h][:, t * P:(t + 1) * P],
                                             LF[:, 4 * j + h:4 * j + h + 1].to_broadcast([P, P]),
                                             cst("uall" if j == t else "ones"), start=j == 0, stop=j == t)
                    last.then_inc(S("fox_cum"), 1)

                def fox_scores(n):
                    h, b = n // 4, n % 4
                    r, q, w = half(h), h // 2, (b + 1) * P
                    need(pe, S("fox_a"), n - 1)
                    pe.matmul(ps[n % 2][:, 0:w], FQ[r, q, b * P:w], FK[r, q, 0:w], start=True, stop=False,
                              skip_group_check=True)
                    pe.matmul(ps[n % 2][:, b * P:w], cst("ident"), cst("neginc"), start=False, stop=True,
                              skip_group_check=True).then_inc(S("fox_s"), 1)

                def fox_turn(n):
                    pe.wait_ge(S("fox_p"), n + 1)
                    need(pe, S("fox_pt"), n - 1)
                    for s in range(n % 4 + 1):
                        last = pe.transpose(ps[2 + n % 2][:, s * P:(s + 1) * P], T[:, 2 + n % 2, s * P:(s + 1) * P],
                                            cst("ident"))
                    last.then_inc(S("fox_t"), 1)

                def fox_values(n):
                    h, b = n // 4, n % 4
                    pe.wait_ge(S("fox_pt"), n + 1)
                    for s in range(b + 1):
                        last = pe.matmul(ps[4 + h // 2][half(h), b * P:(b + 1) * P], V[:, s, 64 * h:64 * h + 64],
                                         PT[:, n % 2, s * P:(s + 1) * P], start=s == 0, stop=s == b)
                    last.then_inc(S("fox_o"), 1)

                pe.wait_ge(S("fox_cumb"), H)
                for n in range(16 + 2):
                    if n < 16:
                        fox_scores(n)
                    if 1 <= n <= 16:
                        fox_turn(n - 1)
                    if n >= 2:
                        fox_values(n - 2)

                pe.wait_ge(S("yb_lo"), 2)
                for h in range(H):
                    r, q, b = half(h), h // 2, 3 * (h % 2)
                    need(pe, S("gdn_l"), h - 1)
                    for t in range(TT):
                        tok = slice(t * P, (t + 1) * P)
                        pe.matmul(ps[b][:, tok], C6[r, 2 + q, tok], C6[r, 2 + q, tok], start=True, stop=True)
                        pe.matmul(ps[b + 1][:, tok], C6[r, 2 + q, tok], C6[r, q, tok], start=True, stop=True)
                        last = pe.matmul(ps[b + 2][:, tok], LD[:, 4 * t + h:4 * t + h + 1].to_broadcast([P, P]),
                                         cst("ublk"), start=True, stop=True)
                    last.then_inc(S("gdn_kk"), 1)

                pe.wait_ge(S("gdn_l"), H)
                for h in range(H):
                    pe.wait_ge(S("gdn_nb"), h + 1)
                    need(pe, S("gdn_xy"), h - 1)
                    for t in range(TT):
                        last = pe.transpose(ps[h % 2][:, t * P:(t + 1) * P], NB[:, h, t * P:(t + 1) * P], cst("ident"))
                    last.then_inc(S("gdn_t0"), 1)
                pe.wait_ge(S("gdn_xy"), H)

                def gdn_q(i):
                    h = i % H
                    pe.wait_ge(S("gdn_nb"), i + H + 1)
                    pe.wait_ge(S("gdn_xy"), i + 1)
                    need(pe, S("gdn_qe"), i - 1)
                    for t in range(TT):
                        tok = slice(t * P, (t + 1) * P)
                        last = pe.matmul(ps[i % 2][:, tok], NB[:, h, tok], Y[:, h, tok], start=True, stop=True)
                    last.then_inc(S("gdn_q"), 1)

                def gdn_xy(i):
                    h = i % H
                    pe.wait_ge(S("gdn_qe"), i + 1)
                    need(pe, S("gdn_xy"), H + i - 1)
                    for t in range(TT):
                        tok = slice(t * P, (t + 1) * P)
                        if i < 4 * H:
                            pe.matmul(ps[2 + i % 2][:, tok], QB[:, h, tok], X[:, h, tok], start=True, stop=True)
                        last = pe.matmul(ps[4 + i % 2][:, tok], X[:, h, tok], QB[:, h, tok], start=True, stop=True)
                    last.then_inc(S("gdn_pxy"), 1)

                for i in range(5 * H + 1):
                    if i < 5 * H:
                        gdn_q(i)
                    if i >= 1:
                        gdn_xy(i - 1)

                pe.wait_ge(S("gdn_xy"), 6 * H)
                for t in range(TT):
                    for h in range(H):
                        tok = slice(t * P, (t + 1) * P)
                        pe.matmul(ps[6 + t // 2][:, ((t % 2) * H + h) * HD:((t % 2) * H + h + 1) * HD],
                                  Y[:, h, tok], VB[:, t * H + h, :], start=True, stop=True)
                        last = pe.matmul(ps[h // 2][half(h), tok], KBE[:, t * H + h, :], Y[:, h, tok],
                                         start=True, stop=True)
                last.then_inc(S("gdn_uw"), 1)
                pe.wait_ge(S("gdn_uwe"), 4)
                for n in range(NC):
                    t, p0 = n // 2, slice(64 * (n % 2), 64 * (n % 2) + 64)
                    tok = slice(64 * n, 64 * n + 64)
                    need(pe, S("gdn_state"), n)
                    for h in range(H):
                        last = pe.matmul(ps[6 * (1 - h % 2)][p0, (h // 2) * HD:(h // 2 + 1) * HD], WT[half(h), h // 2, tok], ST[half(h), h // 2],
                                         start=True, stop=True)
                    last.then_inc(S("gdn_pv"), 1)
                    for h in range(H):
                        pe.matmul(ps[2 + h % 2][p0, (2 * t + h // 2) * HD:(2 * t + h // 2 + 1) * HD],
                                  C6[half(h), h // 2, tok], ST[half(h), h // 2], start=True, stop=True)
                    pe.wait_ge(S("gdn_vn"), n + 1)
                    for h in range(H):
                        last = pe.matmul(ps[7][half(h), (h // 2) * HD:(h // 2 + 1) * HD], KD[p0, t * H + h, :],
                                         VN[p0, h, :], start=True, stop=True)
                    last.then_inc(S("gdn_pk"), 1)
                    for h in range(H):
                        last = pe.matmul(ps[4 + t // 2][p0, ((t % 2) * H + h) * HD:((t % 2) * H + h + 1) * HD],
                                         AT[p0, h, tok], VN[p0, h, :], start=True, stop=True)
                last.then_inc(S("gdn_oo"), 1)
                pe.wait_ge(S("gdn_on"), 1)
                for q in range(2):
                    for t in range(TT):
                        last = pe.transpose(ps[q][:, t * P:(t + 1) * P],
                                            OT[:, t * H + 2 * q:t * H + 2 * q + 2, :].rearrange("p a b -> p (a b)"),
                                            cst("ident"))
                    last.then_inc(S("gdn_ot"), 1)

                pe.wait_ge(S("yd_lo"), 2)
                pe.wait_ge(S("yc_lo"), 2)
                pe.wait_ge(S("ya_lo"), 2)
                for d in range(KT):
                    after(pe, "b", "y", d - 1)
                    pe_block(pe, 0, B_OUT + d, ps[4 + d % 2], XH, XL)
                ln_stats_pe(pe, "b")

                pe.wait_ge(S("mem_lo"), 1)
                for i in range(KT):
                    need(pe, S("mk_evac"), i - 3)
                    pe_block(pe, 0, B_MK + i, ps[i % 4], MTH, MTL, cols=NMEM)
                after(pe, "b", "y", KT)
                for hh in range(2):
                    need(pe, S("mv_evac"), 2 * hh)
                    for i in range(4):
                        c = B_MV + 4 * hh + i
                        pe.wait_ge(split_done, c + 1)
                        for kk in range(2):
                            k = 2 * i + kk
                            w = slice(512 * kk, 512 * kk + 512)
                            for m in range(2):
                                tok = slice(m * P, (m + 1) * P)
                                pe.matmul(ps[4 + m][:], MTH[:, k, tok], WH[:, c % 2, w], start=k == 0, stop=False)
                                pe.matmul(ps[4 + m][:], MTH[:, k, tok], WL[:, c % 2, w], start=False, stop=False)
                                last = pe.matmul(ps[4 + m][:], MTL[:, k, tok], WH[:, c % 2, w], start=False,
                                                 stop=k == KT - 1)
                        last.then_inc(used, 1)
                for i in range(KT):
                    need(pe, S("mq_evac"), i - 3)
                    if i < 4:
                        pe.wait_ge(S("mk_evac"), 5 + i)
                    pe_block(pe, 0, B_MQ + i, ps[i % 4], XH, XL, ready=("b", "xlo") if i == 0 else None)

                def mem_scores(n):
                    h, t = n // 4, n % 4
                    need(pe, S("mem_a"), n - 1)
                    for c in range(2):
                        last = pe.matmul(ps[n % 2][:, 0:NMEM], MQ[:, 2 * h + c, t * P:(t + 1) * P], KM[:, 2 * h + c, :],
                                         start=c == 0, stop=c == 1)
                    last.then_inc(S("mem_s"), 1)

                def mem_turn(n):
                    pe.wait_ge(S("mem_p"), n + 1)
                    need(pe, S("mem_pt"), n - 1)
                    for m in range(2):
                        last = pe.transpose(ps[2 + n % 2][:, m * P:(m + 1) * P], T[:, n % 2, m * P:(m + 1) * P],
                                            cst("ident"))
                    last.then_inc(S("mem_t"), 1)

                def mem_values(h):
                    pe.wait_ge(S("mem_pt"), 4 * h + 4)
                    for c in range(2):
                        need(pe, S("mem_olo"), 2 * h - 1 + c)
                        for m in range(2):
                            last = pe.matmul(ps[4 + c][:], VM[:, m, h * 256 + c * P:h * 256 + (c + 1) * P],
                                             MP[:, h % 2, m, :], start=m == 0, stop=m == 1)
                        last.then_inc(S("mem_o"), 1)

                pe.wait_ge(S("mq_evac"), KT)
                pe.wait_ge(S("mv_evac"), 4)
                for n in range(16 + 2):
                    if n < 16:
                        mem_scores(n)
                    if 1 <= n <= 16:
                        mem_turn(n - 1)
                    if n >= 5 and (n - 5) % 4 == 0:
                        mem_values((n - 5) // 4)
                pe.wait_ge(S("mem_olo"), KT)
                for d in range(KT):
                    after(pe, "c", "y", d - 1)
                    pe_block(pe, 0, B_MO + d, ps[4 + d % 2], XH, XL)
                ln_stats_pe(pe, "c")

                ffn_pe(pe, "d", B_UP2, ("c", "xlo"))

            @block.scalar
            def _(act):
                ffn_act(act, "a", B_UP1, B_IN + 2)
                ln_sqrt_act(act, "a")
                act.wait_ge(S("prm_landed"), 16)
                for d in range(KT + 1):
                    ln_affine_act(act, "a", 0, d)

                def conv_silu(t):
                    act.wait_ge(S("gdn_conv"), 4 * t + 4)
                    act.activation(C6[:, t], C6[:, t], ACT.Silu).then_inc(S("qkv_silu"), 1)

                for i in range(20):
                    split_hi(act, 0, B_IN + i + 2)
                    act.wait_ge(used, B_IN + i + 1)
                    src = ps[i % 4][:]
                    if i < 6:
                        dst, fn, sc = RAW6[:, i, 3:], ACT.Copy, 1.0
                    elif i in (6, 8):
                        act.activation(T[:, (i - 6) // 2], src, ACT.Sigmoid).then_inc(S(f"proj_evac{i % 4}"), 1)
                        dst = None
                    elif i in (7, 9):
                        dst = None
                    elif i < 18:
                        dst = (SQ, SK, FQ, FK)[(i - 10) // 2][:, i % 2, :]
                        fn, sc = ACT.Copy, (0.125 if i in (10, 11, 14, 15) else 1.0)
                    else:
                        dst, fn, sc = ZS[:, i - 18], ACT.Silu, 1.0
                    if dst is not None:
                        act.activation(dst, src, fn, scale=sc).then_inc(S(f"proj_evac{i % 4}"), 1)
                    if i == 1:
                        act.wait_ge(S("gates_abs"), 1)
                        act.activation(AB, AB, ACT.Exp, scale=-1.0).then_inc(S("gates_act"), 1)
                        act.wait_ge(S("gates_act"), 1)
                        act.activation(AB, AB, ACT.Ln, bias=1.0).then_inc(S("gates_act"), 1)
                        act.activation(EB, G.rearrange("p (t c) -> p t c", c=12)[:, :, 4:8], ACT.Exp,
                                       scale=-1.0).then_inc(S("gates_act"), 1)
                        act.activation(EA, prm(P_ALOG, 4), ACT.Exp).then_inc(S("gates_act"), 1)
                    if 2 <= i < 8:
                        conv_silu(i - 2)
                        if i < 6:
                            act.wait_ge(S("qkv_silu"), i - 1)
                            act.activation(T[:, i], C6[:, i - 2], ACT.Square).then_inc(S("qk_sq"), 1)
                    if i == 8:
                        act.wait_ge(S("decays_evac"), 2)
                        act.activation(EG, CUM48[:, 0:16], ACT.Exp).then_inc(S("decay_exp"), 1)
                        act.activation(KDC, KDC, ACT.Exp).then_inc(S("decay_exp"), 1)
                        act.activation(EGL, CUM48[:, 32:48], ACT.Exp).then_inc(S("decay_exp"), 1)
                    if i == 16:
                        for t in range(4):
                            act.wait_ge(S("qk_sum"), t + 1)
                            act.activation(T[:, 2 + t], ps[4 + t][:], ACT.Sqrt, bias=EPS[:, 0:1]).then_inc(
                                S("qk_root"), 1)
                for i in range(4):
                    split_hi(act, 0, B_V + i + 2)
                for t in range(TT):
                    act.wait_ge(used, B_V + 4)
                    act.activation(V[:, t], ps[4 + t][:], ACT.Copy).then_inc(S("v_evac"), 1)
                act.wait_ge(S("dw"), 2 * KDW)
                act.wait_ge(S("qk_norm"), 4)
                for j in range(2):
                    act.activation(T[:, 4 + j], DWA[:, j], ACT.Square).then_inc(S("dw_sq"), 1)
                for j in range(2):
                    act.wait_ge(S("conv_var"), j + 1)
                    act.activation(T[:, 2 + j], T[:, 2 + j], ACT.Sqrt).then_inc(S("conv_sd"), 1)
                for j in range(2):
                    act.wait_ge(S("conv_norm"), 3 + j)
                    act.activation(T[:, j], DWA[:, j], ACT.Silu, bias=prm(P_CNB + j),
                                   scale=prm(P_CNG + j)).then_inc(S("yc"), 1)
                for j in range(2):
                    act.wait_ge(S("yc"), j + 1)
                    act.activation(XH[:, 4 + j], T[:, j], ACT.Copy).then_inc(S("yc_hi"), 1)

                act.wait_ge(S("yc_lo"), 2)
                act.wait_ge(S("conv_norm"), 4)

                def sb_log(h):
                    b = 3 * (h % 2)
                    need(act, S("sb_sp"), 3 * (h - 1))
                    for i, (c0, w) in enumerate(SBW):
                        act.wait_ge(S("sb_z"), 3 * h + i + 1)
                        act.activation(T[:, b + i, :w], ps[b + i][:, :w], ACT.Abs).then_inc(S("sb_abs"), 1)
                    for i, (c0, w) in enumerate(SBW):
                        act.wait_ge(S("sb_abs"), 3 * h + i + 1)
                        act.activation(T[:, b + i, :w], T[:, b + i, :w], ACT.Exp, scale=-1.0).then_inc(S("sb_exp"), 1)
                    for i, (c0, w) in enumerate(SBW):
                        act.wait_ge(S("sb_exp"), 3 * h + i + 1)
                        act.activation(T[:, b + i, :w], T[:, b + i, :w], ACT.Ln, bias=1.0).then_inc(S("sb_ln"), 1)

                def sb_weights(h):
                    need(act, S("sb_o"), h - 1)
                    for i, (c0, w) in enumerate(SBW):
                        act.wait_ge(S("sb_sum"), 3 * h + i + 1)
                        act.activation(SW[:, h % 2, c0:c0 + w], ps[3 * (h % 2) + i][:, :w],
                                       ACT.Exp).then_inc(S("sb_w"), 1)

                sb_log(0)
                sb_log(1)
                for h in range(H):
                    sb_weights(h)
                    if h + 2 < H:
                        sb_log(h + 2)
                for q in range(2):
                    act.wait_ge(S("sb_o"), 2 * q + 2)
                    act.activation(XH[:, 6 + q], ps[6 + q][:], ACT.Copy).then_inc(S("yd_hi"), 1)

                for h in range(H):
                    act.wait_ge(S("fox_cum"), h + 1)
                    act.activation(CUMB[:, h], ps[h][:], ACT.Copy).then_inc(S("fox_cumb"), 1)
                for n in range(16 + 1):
                    if n < 16:
                        w = (n % 4 + 1) * P
                        act.wait_ge(S("fox_m"), n + 1)
                        need(act, S("fox_t"), n - 1)
                        act.activation(T[:, 2 + n % 2, :w], T[:, n % 2, :w], ACT.Exp, bias=NM[:, n:n + 1],
                                       accum_out=RS[:, n:n + 1]).then_inc(S("fox_e"), 1)
                    if n >= 1:
                        m = n - 1
                        w = (m % 4 + 1) * P
                        act.wait_ge(S("fox_t"), m + 1)
                        need(act, S("fox_o"), m - 1)
                        act.activation(PT[:, m % 2, :w], ps[2 + m % 2][:, :w], ACT.Copy).then_inc(S("fox_pt"), 1)
                for q in range(2):
                    act.wait_ge(S("fox_o"), 8 * q + 8)
                    act.activation(XH[:, 2 + q], ps[4 + q][:], ACT.Copy).then_inc(S("yb_hi"), 1)

                for h in range(H):
                    b = 3 * (h % 2)
                    act.wait_ge(S("gdn_clip"), 2 * h + 1)
                    act.activation(T[:, b + 1], T[:, b + 1], ACT.Exp).then_inc(S("gdn_exp"), 1)
                    act.wait_ge(S("gdn_clip"), 2 * h + 2)
                    act.activation(T[:, b + 2], T[:, b + 2], ACT.Exp, scale=-1.0).then_inc(S("gdn_exp"), 1)
                for i in range(5 * H):
                    act.wait_ge(S("gdn_q"), i + 1)
                    need(act, S("gdn_pxy"), i - 3)
                    act.activation(QB[:, i % H], ps[i % 2][:], ACT.Copy).then_inc(S("gdn_qe"), 1)
                act.wait_ge(S("gdn_uw"), 1)
                for q in range(2):
                    act.activation(U[:, 8 * q:8 * q + 8, :].rearrange("p a b -> p (a b)"), ps[6 + q][:],
                                   ACT.Copy).then_inc(S("gdn_uwe"), 1)
                for q in range(2):
                    act.activation(WT[:, q], ps[q][:], ACT.Copy).then_inc(S("gdn_uwe"), 1)
                act.wait_ge(S("gdn_o"), 2)
                act.activation(OSQ[:], OT[:], ACT.Square).then_inc(S("gdn_osq"), 1)
                act.wait_ge(S("gdn_ms"), 2)
                act.activation(OS16, OS16, ACT.Sqrt).then_inc(S("gdn_rms"), 1)
                for j in range(2):
                    act.wait_ge(S("ya"), j + 1)
                    act.activation(XH[:, j], T[:, j], ACT.Copy).then_inc(S("ya_hi"), 1)

                for d in range(KT):
                    split_hi(act, 0, B_OUT + 2 + d)
                    ln_square_act(act, "b", d)
                act.wait_ge(S("mem_landed"), 16)
                act.activation(MTH[:], MT[:], ACT.Copy).then_inc(S("mem_hi"), 1)
                for i in range(16):
                    split_hi(act, 0, B_MK + 2 + i)
                    if i < 8:
                        act.wait_ge(used, B_MK + i + 1)
                        act.activation(KM[:, i], ps[i % 4][:, :NMEM], ACT.Copy).then_inc(S("mk_evac"), 1)
                    elif i in (11, 15):
                        hh = (i - 11) // 4
                        act.wait_ge(used, B_MV + 4 * hh + 4)
                        for m in range(2):
                            act.activation(VM[:, m, 512 * hh:512 * hh + 512], ps[4 + m][:],
                                           ACT.Copy).then_inc(S("mv_evac"), 1)
                    if i == 2:
                        ln_sqrt_act(act, "b")
                    if 3 <= i < 12:
                        ln_affine_act(act, "b", 1, i - 3)
                for i in range(KT):
                    split_hi(act, 0, B_MQ + 2 + i)
                    act.wait_ge(used, B_MQ + i + 1)
                    act.activation(MQ[:, i], ps[i % 4][:], ACT.Copy, scale=1.0 / 16).then_inc(S("mq_evac"), 1)

                def mem_out(h):
                    for c in range(2):
                        act.wait_ge(S("mem_o"), 2 * h + c + 1)
                        act.activation(XH[:, 2 * h + c], ps[4 + c][:], ACT.Copy).then_inc(S("mem_ohi"), 1)

                for n in range(16 + 1):
                    if n < 16:
                        act.wait_ge(S("mem_m"), n + 1)
                        need(act, S("mem_t"), n - 1)
                        act.activation(T[:, n % 2, :NMEM], ps[n % 2][:, :NMEM], ACT.Exp, bias=NM[:, n:n + 1],
                                       accum_out=RS[:, n:n + 1]).then_inc(S("mem_a"), 1)
                    if n >= 1:
                        m = n - 1
                        h, t = m // 4, m % 4
                        act.wait_ge(S("mem_t"), m + 1)
                        if h >= 2 and t == 0:
                            act.wait_ge(S("mem_o"), 2 * (h - 2) + 2)
                        act.activation(MP[:, h % 2, :, t * P:(t + 1) * P],
                                       ps[2 + m % 2][:, :NMEM].rearrange("p (a b) -> p a b", a=2),
                                       ACT.Copy).then_inc(S("mem_pt"), 1)
                    if n >= 7 and (n - 7) % 4 == 0:
                        mem_out((n - 7) // 4)
                mem_out(3)
                for d in range(KT):
                    split_hi(act, 0, B_MO + 2 + d)
                    ln_square_act(act, "c", d)
                ln_sqrt_act(act, "c")
                for d in range(KT + 1):
                    ln_affine_act(act, "c", 2, d)

                ffn_act(act, "d", B_UP2, B_END)
                ln_sqrt_act(act, "d")
                for d in range(KT + 1):
                    ln_affine_act(act, "d", 3, d)

            @block.vector
            def _(dve):
                ffn_dve(dve, "a", B_UP1)

                dve.memset(RAW6[:, :, 0:3], 0.0).then_inc(S("pads"), 1)
                dve.memset(GLU[:, :, 0:30], 0.0).then_inc(S("pads"), 1)
                dve.memset(ST, 0.0).then_inc(S("pads"), 1)
                gs = [0]

                def link(ins):
                    gs[0] += 1
                    ins.then_inc(S("gates_chain"), 1)
                    dve.wait_ge(S("gates_chain"), gs[0])

                dve.wait_ge(S("gates"), 1)
                dve.wait_ge(S("prm_landed"), 16)
                dve.tensor_copy(G, ps[4][:, 0:48]).then_inc(S("gates_evac"), 1)
                dve.wait_ge(S("gates_evac"), 1)
                Gv = G.rearrange("p (t c) -> p t c", c=12)
                Uv = U8.rearrange("p (g t c) -> p g t c", g=2, c=4)
                dve.tensor_tensor(Uv[:, 0], Gv[:, :, 0:4], prm(P_DT, 4).unsqueeze(1).to_broadcast([P, 4, 4]), ALU.add)
                link(dve.scalar_tensor_tensor(Uv[:, 1], Gv[:, :, 8:12], -1.0,
                                              prm(P_FB, 4).unsqueeze(1).to_broadcast([P, 4, 4]), ALU.mult,
                                              ALU.subtract))
                dve.scalar_tensor_tensor(AB, U8, -1.0, U8, ALU.mult, ALU.max).then_inc(S("gates_abs"), 1)
                dve.wait_ge(S("gates_act"), 4)
                link(dve.scalar_tensor_tensor(SPL, U8, 0.0, AB, ALU.max, ALU.add))
                link(dve.scalar_tensor_tensor(
                    LD.rearrange("p (t h) -> p t h", h=4), SPL[:, 0:16].rearrange("p (t h) -> p t h", h=4), -1.0,
                    EA.unsqueeze(1).to_broadcast([P, 4, 4]), ALU.mult, ALU.mult))
                link(dve.tensor_scalar(LF, SPL[:, 16:32], -1.0, None, ALU.mult))
                link(dve.tensor_scalar(EB, EB, 1.0, None, ALU.add))
                dve.reciprocal(BETA, EB).then_inc(S("gates_log"), 1)

                dve.wait_ge(S("pads"), 3)
                cv = S("gdn_conv")
                for t in range(6):
                    evac_wait(dve, t)
                    dve.tensor_scalar(C6[:, t], RAW6[:, t, 0:SEQ], prm(P_GCONV + 4 * t), None, ALU.mult).then_inc(cv, 1)
                    for i in range(1, KCONV):
                        dve.wait_ge(cv, 4 * t + i)
                        dve.scalar_tensor_tensor(C6[:, t], RAW6[:, t, i:i + SEQ], prm(P_GCONV + 4 * t + i), C6[:, t],
                                                 ALU.mult, ALU.add).then_inc(cv, 1)
                for j in range(2):
                    evac_wait(dve, 6 + 2 * j)
                    dve.wait_ge(used, B_IN + 8 + 2 * j)
                    dve.tensor_tensor(GLU[:, j, 30:], T[:, j], ps[(7 + 2 * j) % 4][:], ALU.mult).then_inc(
                        S(f"proj_evac{(7 + 2 * j) % 4}"), 1)
                    if j == 0:
                        dve.wait_ge(S("decays"), 1)
                        dve.tensor_copy(CUM48, ps[5][:, 0:48]).then_inc(S("decays_evac"), 1)
                        dve.wait_ge(S("decays_evac"), 1)
                        dve.tensor_tensor(KDC, CUM48[:, 16:32], CUM48[:, 0:16], ALU.subtract).then_inc(
                            S("decays_evac"), 1)
                evac_wait(dve, 7)
                evac_wait(dve, 9)
                for i in range(KDW):
                    for j in range(2):
                        src, w = GLU[:, j, i:i + SEQ], prm(P_DWW + KDW * j + i)
                        if i == 0:
                            ins = dve.tensor_scalar(DWA[:, j], src, w, prm(P_DWB + j), ALU.mult, ALU.add)
                        else:
                            dve.wait_ge(S("dw"), 2 * (i - 1) + j + 1)
                            ins = dve.scalar_tensor_tensor(DWA[:, j], src, w, DWA[:, j], ALU.mult, ALU.add)
                        ins.then_inc(S("dw"), 1)
                dve.wait_ge(S("decay_exp"), 3)
                dve.tensor_tensor(BEG, BETA, EG, ALU.mult)
                dve.tensor_scalar(EG8, EG, 0.125, None, ALU.mult).then_inc(S("coef"), 1)
                for t in range(4):
                    dve.wait_ge(S("qk_root"), t + 1)
                    dve.reciprocal(T[:, 2 + t], T[:, 2 + t]).then_inc(S("qk_inv"), 1)
                    dve.wait_ge(S("qk_inv"), t + 1)
                    dve.tensor_tensor(C6[:, t], C6[:, t], T[:, 2 + t], ALU.mult).then_inc(S("qk_norm"), 1)

                def per_head(q, coef):
                    return coef.rearrange("p (t h) -> p t h", h=4)[:, :, 2 * q:2 * q + 2].unsqueeze(3).to_broadcast(
                        [P, 4, 2, 64])

                def pair_of(ten, q):
                    return ten[:].rearrange("p (t h) d -> p t h d", h=4)[:, :, 2 * q:2 * q + 2, :]

                dve.wait_ge(S("coef"), 1)
                for q in range(2):
                    src = ps[q][:].rearrange("p (t h d) -> p t h d", t=4, h=2)
                    dve.wait_ge(S("kv_tok"), q + 1)
                    dve.tensor_tensor(pair_of(KBE, q), src, per_head(q, BEG), ALU.mult).then_inc(S("kv_scaled"), 1)
                    dve.tensor_tensor(pair_of(KD, q), src, per_head(q, KDC), ALU.mult).then_inc(S("kv_scaled"), 1)
                for q in range(2):
                    src = ps[2 + q][:].rearrange("p (t h d) -> p t h d", t=4, h=2)
                    dve.wait_ge(S("kv_tok"), 3 + q)
                    dve.tensor_tensor(pair_of(VB, q), src, per_head(q, BETA), ALU.mult).then_inc(S("kv_scaled"), 1)

                cs = S("conv_chain")
                for j in range(2):
                    dve.wait_ge(S("dw_sum"), j + 1)
                    dve.tensor_scalar(T[:, j], ps[2 * j][:], 1.0 / 64, None, ALU.mult).then_inc(cs, 1)
                    dve.wait_ge(cs, 4 * j + 1)
                    dve.tensor_tensor(T[:, 4 + j], T[:, j], T[:, j], ALU.mult).then_inc(cs, 1)
                    dve.wait_ge(cs, 4 * j + 2)
                    dve.scalar_tensor_tensor(T[:, 2 + j], ps[2 * j + 1][:], 1.0 / 64, T[:, 4 + j], ALU.mult,
                                             ALU.subtract).then_inc(cs, 1)
                    dve.wait_ge(cs, 4 * j + 3)
                    dve.tensor_scalar(T[:, 2 + j], T[:, 2 + j], 0.0, LN_EPS, ALU.max, ALU.add).then_inc(
                        S("conv_var"), 1)
                    dve.tensor_tensor(DWA[:, j], DWA[:, j], T[:, j], ALU.subtract).then_inc(cs, 1)
                for j in range(2):
                    dve.wait_ge(S("conv_sd"), j + 1)
                    dve.reciprocal(T[:, 2 + j], T[:, 2 + j]).then_inc(S("conv_norm"), 1)
                for j in range(2):
                    dve.wait_ge(S("conv_norm"), 2 + j)
                    dve.wait_ge(cs, 8)
                    dve.tensor_tensor(DWA[:, j], DWA[:, j], T[:, 2 + j], ALU.mult).then_inc(S("conv_norm"), 1)

                for h in range(H):
                    b = 3 * (h % 2)
                    need(dve, S("sb_sum"), 3 * (h - 1))
                    for i, (c0, w) in enumerate(SBW):
                        dve.wait_ge(S("sb_ln"), 3 * h + i + 1)
                        dve.scalar_tensor_tensor(SP[:, h % 2, c0:c0 + w], ps[b + i][:, :w], 0.0, T[:, b + i, :w],
                                                 ALU.max, ALU.add).then_inc(S("sb_sp"), 1)
                        dve.wait_ge(S("sb_sp"), 3 * h + i + 1)
                        diag = SP[:, h % 2, c0:c0 + P]
                        if i == 1:
                            dve.tensor_tensor(diag, diag, cst("mst"), ALU.mult)
                            diag = SP[:, h % 2, 896:1024]
                        dve.tensor_tensor(diag, diag, cst("mst"), ALU.mult).then_inc(S("sb_mask"), 1)
                for q in range(2):
                    dve.wait_ge(S("yd_hi"), q + 1)
                    dve.tensor_tensor(XL[:, 6 + q], ps[6 + q][:], f32(XH[:, 6 + q]), ALU.subtract).then_inc(
                        S("yd_lo"), 1)

                for n in range(16 + 1):
                    if n < 16:
                        h, w = n // 4, (n % 4 + 1) * P
                        dve.wait_ge(S("fox_s"), n + 1)
                        dve.wait_ge(S("fox_cumb"), h + 1)
                        need(dve, S("fox_e"), n - 1)
                        dve.tensor_tensor(T[:, n % 2, :w], ps[n % 2][:, :w], CUMB[:, h, :w], ALU.subtract).then_inc(
                            S("fox_a"), 1)
                        dve.wait_ge(S("fox_a"), n + 1)
                        dve.tensor_reduce(NM[:, n:n + 1], T[:, n % 2, :w], AX.X, ALU.max, negate=True).then_inc(
                            S("fox_m"), 1)
                    if n >= 1:
                        m = n - 1
                        w = (m % 4 + 1) * P
                        dve.wait_ge(S("fox_e"), m + 1)
                        dve.reciprocal(RI[:, m:m + 1], RS[:, m:m + 1]).then_inc(S("fox_r"), 1)
                        dve.wait_ge(S("fox_r"), m + 1)
                        dve.tensor_scalar(T[:, 2 + m % 2, :w], T[:, 2 + m % 2, :w], RI[:, m:m + 1], None,
                                          ALU.mult).then_inc(S("fox_p"), 1)
                for q in range(2):
                    dve.wait_ge(S("yb_hi"), q + 1)
                    dve.tensor_tensor(XL[:, 2 + q], ps[4 + q][:], f32(XH[:, 2 + q]), ALU.subtract).then_inc(
                        S("yb_lo"), 1)

                def tiles(ap):
                    return ap.rearrange("p (t c) -> p t c", t=TT)

                def coef_tile(coef, h):
                    return coef.rearrange("p (t h) -> p t h", h=4)[:, :, h:h + 1].to_broadcast([P, TT, P])

                def mask(n):
                    return cst(n).unsqueeze(1).to_broadcast([P, TT, P])

                gc = S("gdn_chain")
                for h in range(H):
                    b = 3 * (h % 2)
                    dve.wait_ge(S("gdn_kk"), h + 1)
                    dve.tensor_tensor(tiles(T[:, b]), tiles(ps[b + 2][:]), coef_tile(CUM48[:, 0:16], h),
                                      ALU.subtract).then_inc(gc, 1)
                    dve.wait_ge(gc, 4 * h + 1)
                    dve.tensor_scalar(T[:, b + 1], T[:, b], 0.0, None, ALU.min).then_inc(S("gdn_clip"), 1)
                    dve.tensor_scalar(T[:, b + 2], T[:, b], 0.0, None, ALU.max).then_inc(S("gdn_clip"), 1)
                    dve.wait_ge(S("gdn_exp"), 2 * h + 1)
                    dve.tensor_tensor(tiles(T[:, b + 1]), tiles(T[:, b + 1]), mask("mdt"), ALU.mult).then_inc(gc, 1)
                    dve.wait_ge(S("gdn_exp"), 2 * h + 2)
                    dve.tensor_tensor(tiles(T[:, b + 2]), tiles(T[:, b + 2]), mask("ml"), ALU.mult).then_inc(gc, 1)
                    dve.wait_ge(gc, 4 * h + 2)
                    dve.scalar_tensor_tensor(AT[:, h], ps[b + 1][:], 0.125, T[:, b + 1], ALU.mult, ALU.mult).then_inc(
                        S("gdn_at"), 1)
                    dve.wait_ge(gc, 4 * h + 3)
                    dve.tensor_tensor(T[:, b + 2], T[:, b + 2], ps[b][:], ALU.mult).then_inc(gc, 1)
                    dve.wait_ge(gc, 4 * h + 4)
                    dve.tensor_tensor(tiles(L[:, h]), tiles(T[:, b + 2]), coef_tile(BETA, h), ALU.mult).then_inc(
                        S("gdn_l"), 1)
                for h in range(H):
                    dve.wait_ge(S("gdn_nb"), h + 1)
                    dve.wait_ge(S("gdn_t0"), h + 1)
                    dve.tensor_tensor(tiles(X[:, h]), mask("ident"), tiles(NB[:, h]), ALU.subtract)
                    dve.tensor_tensor(tiles(Y[:, h]), mask("ident"), tiles(ps[h % 2][:]), ALU.subtract).then_inc(
                        S("gdn_xy"), 1)
                for i in range(5 * H):
                    h = i % H
                    dve.wait_ge(S("gdn_pxy"), i + 1)
                    dve.wait_ge(S("gdn_xy"), i + 1)
                    if i < 4 * H:
                        dve.tensor_tensor(X[:, h], X[:, h], ps[2 + i % 2][:], ALU.subtract)
                    dve.tensor_tensor(Y[:, h], Y[:, h], ps[4 + i % 2][:], ALU.subtract).then_inc(S("gdn_xy"), 1)
                dve.wait_ge(S("gdn_uwe"), 4)
                for n in range(NC):
                    t, p0 = n // 2, slice(64 * (n % 2), 64 * (n % 2) + 64)
                    dve.wait_ge(S("gdn_pv"), n + 1)
                    for e in range(2):
                        last = dve.tensor_tensor(VN[p0, e:H:2, :], U[p0, t * H + e:t * H + H:2, :],
                                                 ps[6 * (1 - e)][p0, 0:2 * HD].rearrange("p (h d) -> p h d", h=2),
                                                 ALU.subtract)
                    last.then_inc(S("gdn_vn"), 1)
                    dve.wait_ge(S("gdn_pk"), n + 1)
                    dve.scalar_tensor_tensor(ST[:, 0], ST[:, 0], EGL[:, n:n + 1], ps[7][:, 0:HD], ALU.mult, ALU.add)
                    dve.scalar_tensor_tensor(ST[:, 1], ST[:, 1], EGL[:, 8 + n:9 + n], ps[7][:, HD:2 * HD], ALU.mult,
                                             ALU.add).then_inc(S("gdn_state"), 1)
                    dve.wait_ge(S("gdn_state"), n + 1)
                dve.wait_ge(S("gdn_oo"), 1)

                def heads16(ap, n=8):
                    return ap.unsqueeze(2).to_broadcast([P, n, HD])

                for e in range(2):
                    dve.tensor_tensor(T[:, e].rearrange("p (t a d) -> p t a d", t=TT, a=2),
                                      ps[2 + e][:].rearrange("p (t a d) -> p t a d", t=TT, a=2),
                                      EG8.rearrange("p (t h) -> p t h", h=H)[:, :, e:H:2].unsqueeze(3).to_broadcast(
                                          [P, TT, 2, HD]), ALU.mult).then_inc(S("gdn_oq"), 1)
                for tb in range(2):
                    for e in range(2):
                        dve.wait_ge(S("gdn_oq"), e + 1)
                        last = dve.tensor_tensor(
                            OT[:].rearrange("p (t h) d -> p t h d", h=H)[:, 2 * tb:2 * tb + 2, e:H:2, :],
                            T[:, e].rearrange("p (t a d) -> p t a d", t=TT, a=2)[:, 2 * tb:2 * tb + 2],
                            ps[4 + tb][:].rearrange("p (t h d) -> p t h d", t=2, h=H)[:, :, e:H:2, :], ALU.add)
                    last.then_inc(S("gdn_o"), 1)
                dve.wait_ge(S("gdn_osq"), 1)
                dve.tensor_reduce(OS16, OSQ[:], AX.X, ALU.add).then_inc(S("gdn_ms"), 1)
                dve.wait_ge(S("gdn_ms"), 1)
                dve.tensor_scalar(OS16, OS16, 1.0 / HD, RMS_EPS, ALU.mult, ALU.add).then_inc(S("gdn_ms"), 1)
                dve.wait_ge(S("gdn_rms"), 1)
                dve.reciprocal(TMP16, OS16).then_inc(S("gdn_ms"), 1)
                dve.wait_ge(S("gdn_ms"), 3)
                dve.tensor_tensor(OT[:], OT[:], heads16(TMP16, 16), ALU.mult).then_inc(S("gdn_on"), 1)
                for q in range(2):
                    dve.wait_ge(S("gdn_ot"), q + 1)
                    dve.scalar_tensor_tensor(T[:, q], ps[q][:], prm(P_GNG), ZS[:, q], ALU.mult, ALU.mult).then_inc(
                        S("ya"), 1)

                ln_gather_dve(dve, "b", ALPHA, lambda d: B_OUT + d + 1)
                ln_dve(dve, "b", LN_EPS)

                for n in range(16 + 1):
                    if n < 16:
                        dve.wait_ge(S("mem_s"), n + 1)
                        dve.tensor_reduce(NM[:, n:n + 1], ps[n % 2][:, :NMEM], AX.X, ALU.max, negate=True).then_inc(
                            S("mem_m"), 1)
                    if n >= 1:
                        m = n - 1
                        dve.wait_ge(S("mem_a"), m + 1)
                        dve.reciprocal(RI[:, m:m + 1], RS[:, m:m + 1]).then_inc(S("mem_r"), 1)
                        dve.wait_ge(S("mem_r"), m + 1)
                        dve.tensor_scalar(T[:, m % 2, :NMEM], T[:, m % 2, :NMEM], RI[:, m:m + 1], None,
                                          ALU.mult).then_inc(S("mem_p"), 1)
                    if n >= 8 and (n - 8) % 4 == 0:
                        h = (n - 8) // 4
                        for c in range(2):
                            dve.wait_ge(S("mem_ohi"), 2 * h + c + 1)
                            dve.tensor_tensor(XL[:, 2 * h + c], ps[4 + c][:], f32(XH[:, 2 * h + c]),
                                              ALU.subtract).then_inc(S("mem_olo"), 1)
                for c in range(2):
                    dve.wait_ge(S("mem_ohi"), 7 + c)
                    dve.tensor_tensor(XL[:, 6 + c], ps[4 + c][:], f32(XH[:, 6 + c]), ALU.subtract).then_inc(
                        S("mem_olo"), 1)
                ln_gather_dve(dve, "c", ALPHA, lambda d: B_MO + d + 1)
                ln_dve(dve, "c", LN_EPS)

                ffn_dve(dve, "d", B_UP2)

        nums = sorted(s.num for s in sems.values())
        assert nums == list(range(nums[0], nums[0] + len(nums))), nums
        nc.sync.sem_clear(range(nums[0], nums[-1] + 1))
        nc.all_engine_barrier()

    stored = nc.alloc_semaphore("stored")
    with nc.Block() as block:
        @block.sync
        def _(sp):
            sp.dma_start(out, XT[:]).then_inc(stored, 16)
            sp.wait_ge(stored, 16)


def lay_out(inp):
    a = {k: np.asarray(v) for k, v in inp.items()}
    n = DEPTH

    def by_tile(w):
        return w.reshape(n, KT, P, -1, P).transpose(0, 3, 2, 1, 4).reshape(n, -1, P, BW)

    def by_k(w):
        return w.reshape(n, 4, 2, P, 512).transpose(0, 1, 3, 2, 4).reshape(n, 4, P, BW)

    def up(t):
        g, u = by_tile(a[t + "_w_gate"]), by_tile(a[t + "_w_up"])
        return np.stack([g, u], axis=2).reshape(n, 2 * FT, P, BW)

    w = a["w_in"]
    gq, gz, ga, fq, ff, cg, sq = 0, 768, 1024, 1032, 1800, 1804, 2316
    order = [gq, gq + 128, gq + 256, gq + 384, gq + 512, gq + 640,
             cg + 256, cg, cg + 384, cg + 128,
             sq, sq + 128, sq + 256, sq + 384, fq, fq + 128, fq + 256, fq + 384, gz, gz + 128]
    w_feat = by_tile(np.concatenate([w[:, :, c:c + 128] for c in order], axis=2))
    w_v = by_k(np.concatenate([w[:, :, fq + 512:fq + 768], w[:, :, sq + 512:sq + 768]], axis=2))
    kv = a["mem_w_kv"]
    wst = np.concatenate([
        up("ffn1"), w_feat, w_v, by_tile(a["w_out"]), by_tile(kv[:, :, :D]), by_k(kv[:, :, D:D + 512]),
        by_k(kv[:, :, D + 512:]), by_tile(a["mem_w_q"]), by_tile(a["mem_w_o"]), up("ffn2")], axis=1)

    def down(w):
        return w.reshape(n, 2, FT // 2, P, KT, P).transpose(0, 4, 1, 3, 2, 5).reshape(n, 16, P, DW_W)

    wdn = np.concatenate([down(a["ffn1_w_down"]), down(a["ffn2_w_down"])], axis=1)

    prm = np.zeros((n, P, NPRM), np.float32)

    def col(v):
        return v.reshape(n, -1, P).transpose(0, 2, 1)

    for i, t in enumerate(("ffn1", "mix", "mem", "ffn2")):
        prm[:, :, P_LN + 16 * i:P_LN + 16 * i + 8] = col(a[f"ln_{t}_g"])
        prm[:, :, P_LN + 16 * i + 8:P_LN + 16 * i + 16] = col(a[f"ln_{t}_b"])
    prm[:, :, P_GCONV:P_GCONV + 24] = a["gdn_conv_w"].reshape(n, KCONV, 6, P).transpose(0, 3, 2, 1).reshape(n, P, 24)
    prm[:, :, P_DWW:P_DWW + 62] = a["conf_dw_w"].reshape(n, KDW, 2, P).transpose(0, 3, 2, 1).reshape(n, P, 62)
    prm[:, :, P_DWB:P_DWB + 2] = col(a["conf_dw_b"])
    prm[:, :, P_CNG:P_CNG + 2] = col(a["conf_norm_g"])
    prm[:, :, P_CNB:P_CNB + 2] = col(a["conf_norm_b"])
    prm[:, 0:64, P_GNG] = a["gdn_norm_g"]
    prm[:, 64:128, P_GNG] = a["gdn_norm_g"]
    prm[:, :, P_DT:P_DT + 4] = a["gdn_dt_bias"][:, None, :]
    prm[:, :, P_ALOG:P_ALOG + 4] = a["gdn_a_log"][:, None, :]
    prm[:, :, P_FB:P_FB + 4] = a["fox_b_f"][:, None, :]
    wg = np.concatenate([w[:, :, ga:ga + 8], w[:, :, ff:ff + 4]], axis=2)
    prm[:, :, P_GW:] = wg.reshape(n, KT, P, 12).transpose(0, 2, 1, 3).reshape(n, P, KT * 12)

    xt = a["x"][0].T.reshape(KT, P, SEQ).transpose(1, 0, 2)
    mt = a["mem"][0].T.reshape(KT, P, NMEM).transpose(1, 0, 2)
    return {"xt": xt, "memt": mt, "wst": wst, "wdn": wdn, "prm": prm, "cst": constants()}


def kernel(**inputs):
    import concourse.bacc as bacc
    from concourse.bass_utils import run_bass_kernel_spmd

    nc = bacc.Bacc("TRN2", target_bir_lowering=False, num_devices=1)
    arrays = {k: np.ascontiguousarray(v) for k, v in lay_out(inputs).items()}
    aps = [nc.dram_tensor(k, v.shape, F32, kind="ExternalInput").ap() for k, v in arrays.items()]
    out = nc.dram_tensor("out", (P, KT, SEQ), F32, kind="ExternalOutput").ap()
    build_program(nc, *aps, out)
    r = run_bass_kernel_spmd(nc, [arrays], core_ids=[0])
    o = r.results[0]["out"]
    return np.ascontiguousarray(o.transpose(1, 0, 2).reshape(D, SEQ).T[None])
```

```python
import numpy as np
import concourse.bass as bass
from concourse import mybir

P = 128
D, SEQ, DEPTH, FF, NMEM = 1024, 512, 2, 2816, 256
KT = D // P
TT = SEQ // P
FT = FF // P
H, HD = 4, 64
MH = 4
NC = SEQ // 64
ALPHA = float((2 * DEPTH) ** 0.25)
LN_EPS, RMS_EPS, L2_EPS = 1e-5, 1e-6, 1e-6
KCONV, KDW = 4, 31
BW, DW_W = KT * P, (FT // 2) * P

B_UP1 = 0
B_DN1 = B_UP1 + 2 * FT
B_IN = B_DN1 + 16
B_V = B_IN + 20
B_OUT = B_V + 4
B_MK = B_OUT + 8
B_MV = B_MK + 8
B_MQ = B_MV + 8
B_MO = B_MQ + 8
B_UP2 = B_MO + 8
B_DN2 = B_UP2 + 2 * FT
B_END = B_DN2 + 16

F32 = mybir.dt.float32
F32R = mybir.dt.float32r
ALU = mybir.AluOpType
ACT = mybir.ActivationFunctionType
AX = mybir.AxisListType

CNAMES = ["ident", "uall", "ublk", "blk", "nlt", "none", "ones",
          "negst", "neginc", "mdt", "ml", "mst", "lv0", "lv1", "lv2", "lv3", "lv4", "lv5"]
NCST = len(CNAMES) * P
P_LN, P_GCONV, P_DWW, P_DWB, P_CNG, P_CNB, P_GNG, P_DT, P_ALOG, P_FB, P_GW = (
    0, 64, 88, 150, 152, 154, 156, 157, 161, 165, 169)
NPRM = P_GW + KT * 12


def constants():
    i = np.arange(P)
    r, c = np.broadcast_arrays(i[:, None], i[None, :])
    blk = (r // 64) == (c // 64)
    z = {
        "ident": r == c, "uall": r <= c, "ublk": blk & (r <= c), "blk": blk,
        "nlt": -1.0 * (r >= c), "none": -1.0 * (r >= 0), "ones": r >= 0,
        "negst": -1e30 * (r >= c), "neginc": -1e30 * (c > r),
        "mdt": blk & (r <= c), "ml": blk & (c < r), "mst": r < c,
    }
    for k in range(6):
        s = 1 << k
        z[f"lv{k}"] = (r // (2 * s) == c // (2 * s)) & (r % (2 * s) >= s) & (c % (2 * s) < s)
    return np.concatenate([z[n].astype(np.float32) for n in CNAMES], axis=1)


def need(eng, sem, value):
    if not isinstance(value, int) or value > 0:
        eng.wait_ge(sem, value)


def run_blocks(eng, c0, n, body):
    full = n // 4
    if full > 1:
        with eng.Fori(0, full) as g:
            for j in range(4):
                body(g, c0 + j)
    else:
        for j in range(4 * full):
            body(0, c0 + j)
    for j in range(n - 4 * full):
        body(0, c0 + 4 * full + j)


def build_program(nc, xt_in, memt_in, wst, wdn, prm_in, cst_in, out):
    sb = nc.alloc_sbuf_tensor
    XT = sb("x_t", [P, KT, SEQ], F32)
    XH = sb("x_hi", [P, KT, SEQ], F32R)
    XL = sb("x_lo", [P, KT, SEQ], F32R)
    RAW = sb("w_raw", [P, 4, DW_W], F32)
    WH = sb("w_hi", [P, 2, DW_W], F32R)
    WL = sb("w_lo", [P, 2, DW_W], F32R)
    CST = sb("consts", [P, NCST], F32)
    PRM = sb("params", [P, NPRM], F32)
    T = sb("scratch", [P, 6, SEQ], F32)
    SM = sb("small", [P, 576], F32)
    a0 = (nc.sbuf_base + 31) // 32 * 32
    n_arena = min((nc.sbuf_usable_end - a0) // 4 - 8, 23560)
    sb("arena", [P, n_arena], F32)

    def at(name, col, shape, dt=F32):
        size = 1
        for s in shape:
            size *= s
        assert col + size <= n_arena, (name, col + size, n_arena)
        return nc.alloc_sbuf_tensor_at(name, [P] + shape, dt, offset=a0 + 4 * col)

    HH = at("h_hi", 0, [FT, SEQ], F32R)
    HL = at("h_lo", FT * SEQ, [FT, SEQ], F32R)
    RAW6 = at("gdn_raw", 0, [6, SEQ + 3])
    GLU = at("glu", 3096, [2, SEQ + 30])
    C6 = at("gdn_qkv", 4184, [6, SEQ])
    DWA = at("dw_acc", 7256, [2, SEQ])
    ZS = at("silu_z", 8280, [2, SEQ])
    FQ = at("fox_q", 9304, [2, SEQ])
    FK = at("fox_k", 10328, [2, SEQ])
    SQ = at("sb_q", 11352, [2, SEQ])
    SK = at("sb_k", 12376, [2, SEQ])
    V = at("v_tok", 13400, [TT, 512])
    CUMB = at("fox_cum", 15448, [H, SEQ])
    VB = at("v_beta", 17496, [TT * H, HD])
    KBE = at("k_beta_exp", 18520, [TT * H, HD])
    KD = at("k_decayed", 19544, [TT * H, HD])
    SP = at("softplus", 20568, [1280])
    PT = at("fox_p_t", 21848, [2, SEQ])
    SW = at("sb_weights", 0, [1280])
    FP = at("fox_p", 1280, [3, SEQ])
    L = at("gdn_l", 9304, [H, SEQ])
    X = at("gdn_x", 11352, [H, SEQ])
    Y = at("gdn_y", 13400, [H, SEQ])
    AT = at("gdn_a_t", 15448, [H, SEQ])
    NB = at("gdn_n", 20568, [H, SEQ])
    QB = at("gdn_q", 0, [H, SEQ])
    U = at("gdn_u", 2056, [TT * H, HD])
    WT = at("gdn_w_t", 3096, [2, SEQ])
    OT = at("gdn_o", 9304, [TT * H, HD])
    VN = at("gdn_v_new", 10328, [H, HD])
    OSQ = at("gdn_o_squared", 11352, [TT * H, HD])
    MT = at("mem_t", 0, [KT, NMEM])
    MTH = at("mem_hi", 2048, [KT, NMEM], F32R)
    MTL = at("mem_lo", 4096, [KT, NMEM], F32R)
    KM = at("mem_k", 6144, [KT, NMEM])
    VM = at("mem_v", 8192, [2, D])
    MQ = at("mem_q", 10240, [KT, SEQ])
    MP = at("mem_p_t", 14336, [2, 2, SEQ])

    def small(c, n):
        return SM[:, c:c + n]

    G, U8, AB = small(0, 48), small(48, 32), small(80, 32)
    EA, EB, SPL = small(112, 4), small(116, 16), small(132, 32)
    LD, LF, BETA = small(164, 16), small(180, 16), small(196, 16)
    CUM48, EG, KDC = small(212, 48), small(260, 16), small(276, 16)
    BEG, EG8, EGL = small(292, 16), small(308, 16), small(324, 16)
    NM, RS, RI = small(340, 16), small(356, 16), small(372, 16)
    OS16, EPS = small(388, 16), small(404, 4)
    ST = SM[:, 412:540].rearrange("p (a b) -> p a b", a=2)
    TMP16 = small(540, 16)
    LNS, LNV, LNR, LNM = small(556, 8), small(564, 4), small(568, 4), small(572, 4)

    ps = [nc.alloc_psum_tensor(f"bank{i}", [P, 512], F32) for i in range(8)]

    def cst(n, rows=P):
        k = CNAMES.index(n)
        return CST[:, k * P:(k + 1) * P]

    def prm(c, n=1):
        return PRM[:, c:c + n]

    def f32(ap):
        return ap.bitcast(F32)

    load_sem, prep = nc.alloc_semaphore("inputs_landed"), nc.alloc_semaphore("x_split")
    sems = {}

    def S(name):
        if name not in sems:
            sems[name] = nc.alloc_semaphore(name)
        return sems[name]

    per_use = {"y": KT, "ysum": KT - 1, "sq": KT, "qsum": KT - 1, "stats": 1, "ln": 4, "coef": 2, "rows": 2, "cen": KT, "sd": 1,
               "norm": KT, "aff": KT, "xhi": KT, "xlo": KT, "silu": FT, "h": FT, "hh": FT, "hl": FT}

    def base(tag, name):
        return per_use[name] * (("ad" if per_use[name] == FT else "abcd").index(tag))

    def after(eng, tag, name, value):
        if not isinstance(value, int) or value > 0:
            eng.wait_ge(S("each_" + name), base(tag, name) + value)

    landed = [S(f"landed{r}") for r in range(4)]
    hi_done, split_done, used = S("hi_done"), S("split_done"), S("blocks_used")

    def width(c):
        return DW_W if B_DN1 <= c < B_IN or B_DN2 <= c < B_END else BW

    def load_block(sp, li, g, c):
        need(sp, split_done, 4 * g + c - 3)
        if B_DN1 <= c < B_IN:
            src = wdn[li, 4 * g + (c - B_DN1)]
        elif c >= B_DN2:
            src = wdn[li, 4 * g + (c - B_DN2 + 16)]
        else:
            src = wst[li, 4 * g + (c if c < B_DN1 else c - 16)]
        sp.dma_start(RAW[:, c % 4, :width(c)], src).then_inc(landed[c % 4], 16)

    def split_hi(act, g, c):
        act.wait_ge(landed[c % 4], 16 * g + 16 * (c // 4 + 1))
        need(act, used, 4 * g + c - 1)
        act.activation(WH[:, c % 2, :width(c)], RAW[:, c % 4, :width(c)], ACT.Copy).then_inc(hi_done, 1)

    def split_lo(pool, g, c):
        pool.wait_ge(hi_done, 4 * g + c + 1)
        pool.tensor_tensor(WL[:, c % 2, :width(c)], RAW[:, c % 4, :width(c)],
                           f32(WH[:, c % 2, :width(c)]), ALU.subtract).then_inc(split_done, 1)

    def mm3(pe, o, lh, ll, rh, rl, start, stop):
        pe.matmul(o, lh, rh, start=start, stop=False)
        pe.matmul(o, lh, rl, start=False, stop=False)
        return pe.matmul(o, ll, rh, start=False, stop=stop)

    def pe_block(pe, g, c, bank, rh, rl, k0=0, n=KT, total=KT, cols=SEQ, ready=None):
        pe.wait_ge(split_done, 4 * g + c + 1)
        for i in range(n):
            k = k0 + i
            if ready is not None:
                after(pe, *ready, k + 1)
            w = slice(i * P, (i + 1) * P)
            last = mm3(pe, bank[:, :cols], WH[:, c % 2, w], WL[:, c % 2, w], rh[:, k, :], rl[:, k, :],
                       k == 0, k == total - 1)
        last.then_inc(used, 1)

    def pe_first_pair(pe, c, banks, ready, cols=SEQ):
        pe.wait_ge(split_done, c + 2)
        for k in range(KT):
            after(pe, *ready, k + 1)
            w = slice(k * P, (k + 1) * P)
            for i in range(2):
                last = mm3(pe, banks[i][:, :cols], WH[:, (c + i) % 2, w], WL[:, (c + i) % 2, w], XH[:, k, :],
                           XL[:, k, :], k == 0, k == KT - 1)
                if k == KT - 1:
                    last.then_inc(used, 1)

    def ln_gather_dve(dve, tag, scale, ready):
        for d in range(KT):
            dve.wait_ge(used, ready(d))
            dve.scalar_tensor_tensor(XT[:, d], XT[:, d], scale, ps[4 + d % 2][:], ALU.mult,
                                     ALU.add).then_inc(S("each_y"), 1)
            dve.wait_ge(S("each_y"), base(tag, "y") + d + 1)
            if d >= 1:
                after(dve, tag, "ysum", d - 1)
                dve.tensor_tensor(T[:, 0], XT[:, 0] if d == 1 else T[:, 0], XT[:, d],
                                  ALU.add).then_inc(S("each_ysum"), 1)
                dve.wait_ge(S("each_sq"), base(tag, "sq") + d + 1)
                after(dve, tag, "qsum", d - 1)
                dve.tensor_tensor(T[:, 1], T[:, 2] if d == 1 else T[:, 1], T[:, 2 + d % 2],
                                  ALU.add).then_inc(S("each_qsum"), 1)

    def ln_square_act(act, tag, d):
        act.wait_ge(S("each_y"), base(tag, "y") + d + 1)
        if d >= 2:
            act.wait_ge(S("each_qsum"), base(tag, "qsum") + max(1, d - 2))
        act.activation(T[:, 2 + d % 2], XT[:, d], ACT.Square).then_inc(S("each_sq"), 1)

    def ln_stats_pe(pe, tag):
        for i, name in enumerate(("ysum", "qsum")):
            after(pe, tag, name, KT - 1)
            for t in range(TT):
                last = pe.matmul(ps[6][:, 4 * i + t:4 * i + t + 1], T[:, i, t * P:(t + 1) * P], cst("ones")[:, 0:1],
                                 start=True, stop=True)
        last.then_inc(S("each_stats"), 1)

    def ln_rows_pe(pe, tag):
        for i, v in enumerate((LNR, LNM)):
            after(pe, tag, "coef", i + 1)
            for t in range(TT):
                last = pe.matmul(ps[6 + i][:, t * P:(t + 1) * P], v[:, t:t + 1].to_broadcast([P, P]), cst("ident"),
                                 start=True, stop=True)
            last.then_inc(S("each_rows"), 1)

    def ln_dve(dve, tag, eps):
        st, s0 = S("each_ln"), base(tag, "ln")
        after(dve, tag, "stats", 1)
        dve.tensor_scalar(LNS, ps[6][:, 0:8], 1.0 / D, None, ALU.mult).then_inc(st, 1)
        dve.wait_ge(st, s0 + 1)
        dve.tensor_tensor(LNV, LNS[:, 0:4], LNS[:, 0:4], ALU.mult).then_inc(st, 1)
        dve.wait_ge(st, s0 + 2)
        dve.tensor_tensor(LNV, LNS[:, 4:8], LNV, ALU.subtract).then_inc(st, 1)
        dve.wait_ge(st, s0 + 3)
        dve.tensor_scalar(LNV, LNV, 0.0, eps, ALU.max, ALU.add).then_inc(st, 1)
        after(dve, tag, "sd", 1)
        dve.reciprocal(LNR, LNV).then_inc(S("each_coef"), 1)
        after(dve, tag, "coef", 1)
        dve.tensor_tensor(LNM, LNS[:, 0:4], LNR, ALU.mult).then_inc(S("each_coef"), 1)
        after(dve, tag, "rows", 1)
        for d in range(KT + 1):
            if d < KT:
                dve.tensor_tensor(XT[:, d], XT[:, d], ps[6][:], ALU.mult).then_inc(S("each_cen"), 1)
            if d == 1:
                after(dve, tag, "rows", 2)
            if d >= 1:
                after(dve, tag, "cen", d)
                dve.tensor_tensor(XT[:, d - 1], XT[:, d - 1], ps[7][:], ALU.subtract).then_inc(S("each_norm"), 1)

    def ln_sqrt_act(act, tag):
        after(act, tag, "ln", 4)
        act.activation(LNV, LNV, ACT.Sqrt).then_inc(S("each_sd"), 1)

    def ln_affine_act(act, tag, n, d):
        if d < KT:
            act.wait_ge(S("each_norm"), base(tag, "norm") + d + 1)
            act.activation(XT[:, d], XT[:, d], ACT.Identity, bias=prm(P_LN + 16 * n + 8 + d),
                           scale=prm(P_LN + 16 * n + d)).then_inc(S("each_aff"), 1)
        if d >= 1:
            act.wait_ge(S("each_aff"), base(tag, "aff") + d)
            act.activation(XH[:, d - 1], XT[:, d - 1], ACT.Copy).then_inc(S("each_xhi"), 1)

    def ln_lo_pool(pool, tag, d):
        pool.wait_ge(S("each_xhi"), base(tag, "xhi") + d + 1)
        pool.tensor_tensor(XL[:, d], XT[:, d], f32(XH[:, d]), ALU.subtract).then_inc(S("each_xlo"), 1)

    def ffn_pe(pe, tag, b0, ready):
        up, dn = b0, b0 + 2 * FT

        def pair(g, first):
            for j in range(2):
                f = 2 * g + j
                if first and j == 0 and ready is not None:
                    pe_first_pair(pe, up, (ps[0], ps[2]), ready)
                    continue
                if not first:
                    pe.wait_ge(S("each_silu"), base(tag, "silu") + f - 1)
                pe_block(pe, g, up + 2 * j, ps[j], XH, XL)
                if not first:
                    pe.wait_ge(S("each_h"), base(tag, "h") + f - 1)
                pe_block(pe, g, up + 2 * j + 1, ps[2 + j], XH, XL)

        pair(0, True)
        with pe.Fori(1, FT // 2) as g:
            pair(g, False)

        def down(g, first):
            for j in range(2):
                d = 2 * g + j
                if not first:
                    pe.wait_ge(S("each_y"), base(tag, "y") + d - 1)
                for half in range(2):
                    pe_block(pe, g, dn + 2 * j + half, ps[4 + j], HH, HL, k0=half * (FT // 2), n=FT // 2,
                             total=FT, ready=(tag, "hl") if first and j == 0 else None)

        down(0, True)
        with pe.Fori(1, KT // 2) as g:
            down(g, False)
        ln_stats_pe(pe, tag)
        ln_rows_pe(pe, tag)

    def ffn_act(act, tag, b0, nxt):
        up, dn = b0, b0 + 2 * FT
        for c in (up, up + 1):
            if c < 2:
                split_hi(act, 0, c)

        def pair(g, first):
            for j in range(2):
                f = 2 * g + j
                c = up + 2 * j
                split_hi(act, g, c + 2) if not isinstance(g, int) else split_hi(act, 0, 4 * g + c + 2)
                act.wait_ge(used, 4 * g + c + 1)
                if not first:
                    act.wait_ge(S("each_h"), base(tag, "h") + f - 1)
                act.activation(T[:, j], ps[j][:], ACT.Silu).then_inc(S("each_silu"), 1)
                split_hi(act, g, c + 3) if not isinstance(g, int) else split_hi(act, 0, 4 * g + c + 3)

        pair(0, True)
        with act.Fori(1, FT // 2 - 1) as g:
            pair(g, False)
        pair(FT // 2 - 1, False)
        for d in range(KT):
            for c in (dn + 2 * d + 2, dn + 2 * d + 3):
                if c < nxt:
                    split_hi(act, 0, c)
            ln_square_act(act, tag, d)

    def ffn_dve(dve, tag, b0):
        def pair(g, first):
            for j in range(2):
                f = 2 * g + j
                dve.wait_ge(S("each_silu"), base(tag, "silu") + f + 1)
                dve.wait_ge(used, 4 * g + b0 + 2 * j + 2)
                if not first:
                    dve.wait_ge(S("each_hl"), base(tag, "hl") + f - 1)
                dve.tensor_tensor(T[:, 2 + j], T[:, j], ps[2 + j][:], ALU.mult).then_inc(S("each_h"), 1)
                dve.wait_ge(S("each_h"), base(tag, "h") + f + 1)
                dve.tensor_copy(HH[:, f], T[:, 2 + j]).then_inc(S("each_hh"), 1)
                dve.wait_ge(S("each_hh"), base(tag, "hh") + f + 1)
                dve.tensor_tensor(HL[:, f], T[:, 2 + j], f32(HH[:, f]), ALU.subtract).then_inc(S("each_hl"), 1)

        pair(0, True)
        with dve.Fori(1, FT // 2) as g:
            pair(g, False)
        dn = b0 + 2 * FT
        ln_gather_dve(dve, tag, 2.0 * ALPHA, lambda d: dn + 2 * d + 2)
        ln_dve(dve, tag, 4.0 * LN_EPS)

    def half(h):
        return slice(64 * (h % 2), 64 * (h % 2) + 64)

    SBB = [(0, 0, 512), (1, 0, 384), (2, 0, 256), (1, 384, 128)]
    SBO = [0, 512, 1024, 896]
    SBW = [(0, 512), (512, 512), (1024, 256)]

    MSB = (0, 1, 6)

    def evac_wait(eng, i):
        eng.wait_ge(S(f"proj_evac{i % 4}"), i // 4 + 1)

    with nc.Block() as block:
        @block.sync
        def _(sp):
            sp.dma_start(XT[:], xt_in).then_inc(load_sem, 16)
            sp.dma_start(CST[:], cst_in).then_inc(load_sem, 16)
            sp.wait_ge(load_sem, 32)

        @block.vector
        def _(dve):
            for i, v in enumerate((L2_EPS, LN_EPS, RMS_EPS, 0.0)):
                dve.memset(EPS[:, i:i + 1], v)
            dve.wait_ge(load_sem, 32)
            dve.tensor_copy(XH[:], XT[:]).then_inc(prep, 1)
            dve.wait_ge(prep, 1)
            dve.tensor_tensor(XL[:], XT[:], f32(XH[:]), ALU.subtract).then_inc(prep, 1)
            dve.wait_ge(prep, 2)

    with nc.Fori(0, DEPTH) as li:
        with nc.Block() as block:
            @block.sync
            def _(sp):
                sp.dma_start(PRM[:], prm_in[li]).then_inc(S("prm_landed"), 16)
                for c in range(4):
                    load_block(sp, li, 0, c)
                run_blocks(sp, 4, B_DN1 - 4, lambda g, c: load_block(sp, li, g, c))
                run_blocks(sp, B_DN1, 16, lambda g, c: load_block(sp, li, g, c))
                run_blocks(sp, B_IN, B_OUT + 4 - B_IN, lambda g, c: load_block(sp, li, g, c))
                sp.wait_ge(used, B_OUT + 1)
                sp.dma_start(MT[:], memt_in).then_inc(S("mem_landed"), 16)
                run_blocks(sp, B_OUT + 4, B_DN2 - B_OUT - 4, lambda g, c: load_block(sp, li, g, c))
                run_blocks(sp, B_DN2, 16, lambda g, c: load_block(sp, li, g, c))

            @block.gpsimd
            def _(pool):
                def lo(c0, c1):
                    run_blocks(pool, c0, c1 - c0, lambda g, c: split_lo(pool, g, c))

                lo(0, B_DN1)
                lo(B_DN1, B_IN)
                lo(B_IN, B_IN + 2)
                for d in range(KT):
                    ln_lo_pool(pool, "a", d)
                lo(B_IN + 2, B_OUT + 2)
                for j in range(2):
                    pool.wait_ge(S("yc_hi"), j + 1)
                    pool.tensor_tensor(XL[:, 4 + j], T[:, j], f32(XH[:, 4 + j]), ALU.subtract).then_inc(S("yc_lo"), 1)
                for i in range(6 * H):
                    k, h = i // H, i % H
                    pool.wait_ge(S("gdn_l"), h + 1)
                    if i >= H:
                        if k == 1:
                            pool.wait_ge(S("gdn_t0"), h + 1)
                            pool.wait_ge(S("gdn_xy"), h + 1)
                        else:
                            pool.wait_ge(S("gdn_q"), i - 2 * H + 1)
                    pool.tensor_tensor(
                        NB[:, h].rearrange("p (t c) -> p t c", t=TT), L[:, h].rearrange("p (t c) -> p t c", t=TT),
                        cst(f"lv{k}").unsqueeze(1).to_broadcast([P, TT, P]), ALU.mult).then_inc(S("gdn_nb"), 1)
                for j in range(2):
                    pool.wait_ge(S("ya_hi"), j + 1)
                    pool.tensor_tensor(XL[:, j], T[:, j], f32(XH[:, j]), ALU.subtract).then_inc(S("ya_lo"), 1)
                lo(B_OUT + 2, B_MK + 2)
                pool.wait_ge(S("mem_hi"), 1)
                pool.tensor_tensor(MTL[:], MT[:], f32(MTH[:]), ALU.subtract).then_inc(S("mem_lo"), 1)
                for i in range(16):
                    split_lo(pool, 0, B_MK + 2 + i)
                    if 4 <= i < 12:
                        ln_lo_pool(pool, "b", i - 4)
                lo(B_MQ + 2, B_MO + 2)
                lo(B_MO + 2, B_UP2 + 2)
                for d in range(KT):
                    ln_lo_pool(pool, "c", d)
                lo(B_UP2 + 2, B_DN2)
                lo(B_DN2, B_END)
                for d in range(KT):
                    ln_lo_pool(pool, "d", d)

            @block.tensor
            def _(pe):
                ffn_pe(pe, "a", B_UP1, None)

                pe_first_pair(pe, B_IN, ps[0:2], ("a", "xlo"))
                after(pe, "a", "aff", KT)
                for t in range(TT):
                    for k in range(KT):
                        last = pe.matmul(ps[4][:, 12 * t:12 * t + 12], XT[:, k, t * P:(t + 1) * P],
                                         PRM[:, P_GW + 12 * k:P_GW + 12 * k + 12], start=k == 0, stop=k == KT - 1)
                last.then_inc(S("gates"), 1)

                for i in range(2, 20):
                    if i >= 4:
                        evac_wait(pe, i - 4)
                    pe_block(pe, 0, B_IN + i, ps[i % 4], XH, XL)
                    if i == 6:
                        pe.wait_ge(S("gates_log"), 1)
                        pe.matmul(ps[5][:, 0:16], cst("ublk"), LD, start=True, stop=True)
                        pe.matmul(ps[5][:, 16:32], cst("blk"), LD, start=True, stop=True)
                        for h in range(H):
                            for t in range(TT):
                                c = 32 + 8 * (h // 2) + 2 * t
                                last = pe.matmul(ps[5][half(h), c:c + 2],
                                                 LD[:, 4 * t + h:4 * t + h + 1].to_broadcast([P, 64]),
                                                 cst("blk")[:, 0:P:64], start=True, stop=True)
                        last.then_inc(S("decays"), 1)
                    if i == 15:
                        pe.wait_ge(S("gates_evac"), 1)
                        pe.wait_ge(S("decays_evac"), 1)
                        for t in range(4):
                            pe.wait_ge(S("qk_sq"), t + 1)
                            pe.matmul(ps[4 + t][:], cst("blk"), T[:, 2 + t], start=True,
                                      stop=True).then_inc(S("qk_sum"), 1)
                pe.wait_ge(S("qk_root"), 4)
                for i in range(4):
                    c = B_V + i
                    pe.wait_ge(split_done, c + 1)
                    for kk in range(2):
                        k = 2 * i + kk
                        w = slice(512 * kk, 512 * kk + 512)
                        for t in range(TT):
                            tok = slice(t * P, (t + 1) * P)
                            pe.matmul(ps[4 + t][:], XH[:, k, tok], WH[:, c % 2, w], start=k == 0, stop=False)
                            pe.matmul(ps[4 + t][:], XH[:, k, tok], WL[:, c % 2, w], start=False, stop=False)
                            last = pe.matmul(ps[4 + t][:], XL[:, k, tok], WH[:, c % 2, w], start=False,
                                             stop=k == KT - 1)
                    last.then_inc(used, 1)

                for i in range(16, 20):
                    evac_wait(pe, i)
                for q in range(2):
                    pe.wait_ge(S("qk_norm"), 3 + q)
                    for t in range(TT):
                        last = pe.transpose(ps[q][:, t * P:(t + 1) * P], C6[:, 2 + q, t * P:(t + 1) * P], cst("ident"))
                    last.then_inc(S("kv_tok"), 1)
                pe.wait_ge(S("qkv_silu"), 6)
                for q in range(2):
                    for t in range(TT):
                        last = pe.transpose(ps[2 + q][:, t * P:(t + 1) * P], C6[:, 4 + q, t * P:(t + 1) * P],
                                            cst("ident"))
                    last.then_inc(S("kv_tok"), 1)
                pe.wait_ge(S("kv_scaled"), 6)
                pe.wait_ge(S("dw"), 2 * KDW)
                for j in range(2):
                    pe.matmul(ps[2 * j][:], cst("blk"), DWA[:, j], start=True, stop=True)
                    pe.wait_ge(S("dw_sq"), j + 1)
                    pe.matmul(ps[2 * j + 1][:], cst("blk"), T[:, 4 + j], start=True, stop=True).then_inc(S("dw_sum"), 1)

                pe.wait_ge(S("v_evac"), TT)
                for h in range(H):
                    for t in range(TT):
                        for j in range(t + 1):
                            last = pe.matmul(ps[4 + h][:, t * P:(t + 1) * P],
                                             LF[:, 4 * j + h:4 * j + h + 1].to_broadcast([P, P]),
                                             cst("uall" if j == t else "ones"), start=j == 0, stop=j == t)
                    last.then_inc(S("fox_cum"), 1)

                def sb_scores(h):
                    r, q = half(h), h // 2
                    need(pe, S("sb_w"), 3 * h)
                    for sblk in (0, 1, 3, 2):
                        bank, c0, w = SBB[sblk]
                        pe.matmul(ps[bank][:, c0:c0 + w], SK[r, q, sblk * P:(sblk + 1) * P],
                                  SQ[r, q, sblk * P:], start=c0 == 0, stop=False, skip_group_check=True)
                        last = pe.matmul(ps[bank][:, c0:c0 + P], cst("ident"), cst("negst"), start=False, stop=True,
                                         skip_group_check=True)
                        if sblk != 1:
                            last.then_inc(S("sb_z"), 1)

                def sb_sums(h):
                    pe.wait_ge(S("sb_sp"), 3 * h + 3)
                    for sblk in (0, 1, 3, 2):
                        bank, c0, w = SBB[sblk]
                        o = ps[bank]
                        for j in range(sblk, 4):
                            last = pe.matmul(o[:, c0 + (j - sblk) * P:c0 + w], cst("nlt" if j == sblk else "none"),
                                             SP[:, SBO[j]:SBO[j] + SEQ - j * P], start=False, stop=j == 3,
                                             skip_group_check=True)
                        if sblk != 1:
                            last.then_inc(S("sb_sum"), 1)

                def sb_values(h):
                    pe.wait_ge(S("sb_w"), 3 * h + 3)
                    if h == 2:
                        pe.wait_ge(S("yd_lo"), 1)
                    for s in range(4):
                        last = pe.matmul(ps[3][half(h), s * P:], V[:, s, 256 + 64 * h:256 + 64 * h + 64],
                                         SW[:, SBO[s]:SBO[s] + SEQ - s * P], start=s == 0, stop=s == 3,
                                         skip_group_check=True)
                    last.then_inc(S("sb_o"), 1)

                def fox_scores(n):
                    h, b = n // 4, n % 4
                    r, q, w = half(h), h // 2, (b + 1) * P
                    need(pe, S("fox_a"), n - 1)
                    pe.matmul(ps[4 + n % 2][:, 0:w], FQ[r, q, b * P:w], FK[r, q, 0:w], start=True, stop=False,
                              skip_group_check=True)
                    pe.matmul(ps[4 + n % 2][:, b * P:w], cst("ident"), cst("neginc"), start=False, stop=True,
                              skip_group_check=True).then_inc(S("fox_s"), 1)

                def fox_turn(n):
                    pe.wait_ge(S("fox_p"), n + 1)
                    need(pe, S("fox_pt"), n)
                    for s in range(n % 4 + 1):
                        last = pe.transpose(ps[6][:, s * P:(s + 1) * P], FP[:, n % 3, s * P:(s + 1) * P], cst("ident"))
                    last.then_inc(S("fox_t"), 1)

                def fox_values(n):
                    h, b = n // 4, n % 4
                    pe.wait_ge(S("fox_pt"), n + 1)
                    if n == 8:
                        pe.wait_ge(S("yb_lo"), 1)
                    for s in range(b + 1):
                        last = pe.matmul(ps[7][half(h), b * P:(b + 1) * P], V[:, s, 64 * h:64 * h + 64],
                                         PT[:, n % 2, s * P:(s + 1) * P], start=s == 0, stop=s == b)
                    last.then_inc(S("fox_o"), 1)

                pe.wait_ge(S("conv_norm"), 4)
                for n in range(16 + 3):
                    h, s = n // 4, n % 4
                    if s == 0 and h < H:
                        sb_scores(h)
                        if h == 0:
                            pe.wait_ge(S("fox_cumb"), H)
                    if s == 0 and h >= 1:
                        sb_values(h - 1)
                    if s == 2 and h < H:
                        sb_sums(h)
                    if n < 16:
                        fox_scores(n)
                    if 2 <= n < 16 + 2:
                        fox_turn(n - 2)
                    if n >= 3:
                        fox_values(n - 3)

                pe.wait_ge(S("yb_lo"), 2)
                pe.wait_ge(S("yd_lo"), 2)
                for h in range(H):
                    r, q, b = half(h), h // 2, 3 * (h % 2)
                    need(pe, S("gdn_l"), h - 1)
                    for t in range(TT):
                        tok = slice(t * P, (t + 1) * P)
                        pe.matmul(ps[b][:, tok], C6[r, 2 + q, tok], C6[r, 2 + q, tok], start=True, stop=True)
                        pe.matmul(ps[b + 1][:, tok], C6[r, 2 + q, tok], C6[r, q, tok], start=True, stop=True)
                        last = pe.matmul(ps[b + 2][:, tok], LD[:, 4 * t + h:4 * t + h + 1].to_broadcast([P, P]),
                                         cst("ublk"), start=True, stop=True)
                    last.then_inc(S("gdn_kk"), 1)

                pe.wait_ge(S("gdn_l"), H)
                for h in range(H):
                    pe.wait_ge(S("gdn_nb"), h + 1)
                    need(pe, S("gdn_xy"), h - 1)
                    for t in range(TT):
                        last = pe.transpose(ps[h % 2][:, t * P:(t + 1) * P], NB[:, h, t * P:(t + 1) * P], cst("ident"))
                    last.then_inc(S("gdn_t0"), 1)
                pe.wait_ge(S("gdn_xy"), H)

                def gdn_q(i):
                    h = i % H
                    pe.wait_ge(S("gdn_nb"), i + H + 1)
                    pe.wait_ge(S("gdn_xy"), i + 1)
                    need(pe, S("gdn_qe"), i - 1)
                    for t in range(TT):
                        tok = slice(t * P, (t + 1) * P)
                        last = pe.matmul(ps[i % 2][:, tok], NB[:, h, tok], Y[:, h, tok], start=True, stop=True)
                    last.then_inc(S("gdn_q"), 1)

                def gdn_xy(i):
                    h = i % H
                    pe.wait_ge(S("gdn_qe"), i + 1)
                    need(pe, S("gdn_xy"), H + i - 1)
                    for t in range(TT):
                        tok = slice(t * P, (t + 1) * P)
                        if i < 4 * H:
                            pe.matmul(ps[2 + i % 2][:, tok], QB[:, h, tok], X[:, h, tok], start=True, stop=True)
                        last = pe.matmul(ps[4 + i % 2][:, tok], X[:, h, tok], QB[:, h, tok], start=True, stop=True)
                    last.then_inc(S("gdn_pxy"), 1)

                for i in range(5 * H + 1):
                    if i < 5 * H:
                        gdn_q(i)
                    if i >= 1:
                        gdn_xy(i - 1)

                pe.wait_ge(S("gdn_xy"), 6 * H)
                for t in range(TT):
                    for h in range(H):
                        tok = slice(t * P, (t + 1) * P)
                        pe.matmul(ps[6 + t // 2][:, ((t % 2) * H + h) * HD:((t % 2) * H + h + 1) * HD],
                                  Y[:, h, tok], VB[:, t * H + h, :], start=True, stop=True)
                        last = pe.matmul(ps[h // 2][half(h), tok], KBE[:, t * H + h, :], Y[:, h, tok],
                                         start=True, stop=True)
                last.then_inc(S("gdn_uw"), 1)
                pe.wait_ge(S("gdn_uwe"), 4)
                for n in range(NC):
                    t, p0 = n // 2, slice(64 * (n % 2), 64 * (n % 2) + 64)
                    tok = slice(64 * n, 64 * n + 64)
                    need(pe, S("gdn_state"), n)
                    for h in range(H):
                        last = pe.matmul(ps[6 * (1 - h % 2)][p0, (h // 2) * HD:(h // 2 + 1) * HD], WT[half(h), h // 2, tok], ST[half(h), h // 2],
                                         start=True, stop=True)
                    last.then_inc(S("gdn_pv"), 1)
                    for h in range(H):
                        pe.matmul(ps[2 + h % 2][p0, (2 * t + h // 2) * HD:(2 * t + h // 2 + 1) * HD],
                                  C6[half(h), h // 2, tok], ST[half(h), h // 2], start=True, stop=True)
                    pe.wait_ge(S("gdn_vn"), n + 1)
                    for h in range(H):
                        last = pe.matmul(ps[7][half(h), (h // 2) * HD:(h // 2 + 1) * HD], KD[p0, t * H + h, :],
                                         VN[p0, h, :], start=True, stop=True)
                    last.then_inc(S("gdn_pk"), 1)
                    for h in range(H):
                        last = pe.matmul(ps[4 + t // 2][p0, ((t % 2) * H + h) * HD:((t % 2) * H + h + 1) * HD],
                                         AT[p0, h, tok], VN[p0, h, :], start=True, stop=True)
                last.then_inc(S("gdn_oo"), 1)
                pe.wait_ge(S("gdn_on"), 1)
                for q in range(2):
                    for t in range(TT):
                        last = pe.transpose(ps[q][:, t * P:(t + 1) * P],
                                            OT[:, t * H + 2 * q:t * H + 2 * q + 2, :].rearrange("p a b -> p (a b)"),
                                            cst("ident"))
                    last.then_inc(S("gdn_ot"), 1)

                pe.wait_ge(S("yd_lo"), 2)
                pe.wait_ge(S("yc_lo"), 2)
                pe.wait_ge(S("ya_lo"), 2)
                for d in range(KT):
                    after(pe, "b", "y", d - 1)
                    pe_block(pe, 0, B_OUT + d, ps[4 + d % 2], XH, XL)
                ln_stats_pe(pe, "b")

                pe.wait_ge(S("mem_lo"), 1)
                for i in range(KT):
                    if i == 2:
                        ln_rows_pe(pe, "b")
                    need(pe, S("mk_evac"), i - 3)
                    pe_block(pe, 0, B_MK + i, ps[i % 4], MTH, MTL, cols=NMEM)
                after(pe, "b", "y", KT)
                for hh in range(2):
                    need(pe, S("mv_evac"), 2 * hh)
                    for i in range(4):
                        c = B_MV + 4 * hh + i
                        pe.wait_ge(split_done, c + 1)
                        for kk in range(2):
                            k = 2 * i + kk
                            w = slice(512 * kk, 512 * kk + 512)
                            for m in range(2):
                                tok = slice(m * P, (m + 1) * P)
                                pe.matmul(ps[4 + m][:], MTH[:, k, tok], WH[:, c % 2, w], start=k == 0, stop=False)
                                pe.matmul(ps[4 + m][:], MTH[:, k, tok], WL[:, c % 2, w], start=False, stop=False)
                                last = pe.matmul(ps[4 + m][:], MTL[:, k, tok], WH[:, c % 2, w], start=False,
                                                 stop=k == KT - 1)
                        last.then_inc(used, 1)
                for i in range(KT):
                    need(pe, S("mq_evac"), i - 3)
                    if i < 4:
                        pe.wait_ge(S("mk_evac"), 5 + i)
                    pe_block(pe, 0, B_MQ + i, ps[i % 4], XH, XL, ready=("b", "xlo") if i == 0 else None)

                def mem_scores(n):
                    h, t = n // 4, n % 4
                    need(pe, S("mem_a"), n - 2)
                    for c in range(2):
                        last = pe.matmul(ps[MSB[n % 3]][:, 0:NMEM], MQ[:, 2 * h + c, t * P:(t + 1) * P], KM[:, 2 * h + c, :],
                                         start=c == 0, stop=c == 1)
                    last.then_inc(S("mem_s"), 1)

                def mem_turn(n):
                    pe.wait_ge(S("mem_p"), n + 1)
                    need(pe, S("mem_pt"), n - 1)
                    for m in range(2):
                        last = pe.transpose(ps[2 + n % 2][:, m * P:(m + 1) * P], T[:, n % 3, m * P:(m + 1) * P],
                                            cst("ident"))
                    last.then_inc(S("mem_t"), 1)

                def mem_values(h):
                    pe.wait_ge(S("mem_pt"), 4 * h + 4)
                    for c in range(2):
                        need(pe, S("mem_olo"), 2 * h - 1 + c)
                        for m in range(2):
                            last = pe.matmul(ps[4 + c][:], VM[:, m, h * 256 + c * P:h * 256 + (c + 1) * P],
                                             MP[:, h % 2, m, :], start=m == 0, stop=m == 1)
                        last.then_inc(S("mem_o"), 1)

                pe.wait_ge(S("mq_evac"), KT)
                pe.wait_ge(S("mv_evac"), 4)
                for n in range(16 + 3):
                    if n < 16:
                        mem_scores(n)
                    if 2 <= n < 16 + 2:
                        mem_turn(n - 2)
                    if n >= 6 and (n - 6) % 4 == 0:
                        mem_values((n - 6) // 4)
                pe.wait_ge(S("mem_olo"), KT)
                for d in range(KT):
                    after(pe, "c", "y", d - 1)
                    pe_block(pe, 0, B_MO + d, ps[4 + d % 2], XH, XL)
                ln_stats_pe(pe, "c")
                ln_rows_pe(pe, "c")

                ffn_pe(pe, "d", B_UP2, ("c", "xlo"))

            @block.scalar
            def _(act):
                ffn_act(act, "a", B_UP1, B_IN + 2)
                ln_sqrt_act(act, "a")
                act.wait_ge(S("prm_landed"), 16)
                for d in range(KT + 1):
                    ln_affine_act(act, "a", 0, d)

                def conv_silu(t):
                    act.wait_ge(S("gdn_conv"), 4 * t + 4)
                    act.activation(C6[:, t], C6[:, t], ACT.Silu).then_inc(S("qkv_silu"), 1)

                for i in range(20):
                    split_hi(act, 0, B_IN + i + 2)
                    act.wait_ge(used, B_IN + i + 1)
                    src = ps[i % 4][:]
                    if i < 6:
                        dst, fn, sc = RAW6[:, i, 3:], ACT.Copy, 1.0
                    elif i in (6, 8):
                        act.activation(T[:, (i - 6) // 2], src, ACT.Sigmoid).then_inc(S(f"proj_evac{i % 4}"), 1)
                        dst = None
                    elif i in (7, 9):
                        dst = None
                    elif i < 18:
                        dst = (SQ, SK, FQ, FK)[(i - 10) // 2][:, i % 2, :]
                        fn, sc = ACT.Copy, (0.125 if i in (10, 11, 14, 15) else 1.0)
                    else:
                        dst, fn, sc = ZS[:, i - 18], ACT.Silu, 1.0
                    if dst is not None:
                        act.activation(dst, src, fn, scale=sc).then_inc(S(f"proj_evac{i % 4}"), 1)
                    if i == 1:
                        act.wait_ge(S("gates_abs"), 1)
                        act.activation(AB, AB, ACT.Exp, scale=-1.0).then_inc(S("gates_act"), 1)
                        act.wait_ge(S("gates_act"), 1)
                        act.activation(AB, AB, ACT.Ln, bias=1.0).then_inc(S("gates_act"), 1)
                        act.activation(EB, G.rearrange("p (t c) -> p t c", c=12)[:, :, 4:8], ACT.Exp,
                                       scale=-1.0).then_inc(S("gates_act"), 1)
                        act.activation(EA, prm(P_ALOG, 4), ACT.Exp).then_inc(S("gates_act"), 1)
                    if 2 <= i < 8:
                        conv_silu(i - 2)
                        if i < 6:
                            act.wait_ge(S("qkv_silu"), i - 1)
                            act.activation(T[:, i], C6[:, i - 2], ACT.Square).then_inc(S("qk_sq"), 1)
                    if i == 8:
                        act.wait_ge(S("decays_evac"), 2)
                        act.activation(EG, CUM48[:, 0:16], ACT.Exp).then_inc(S("decay_exp"), 1)
                        act.activation(KDC, KDC, ACT.Exp).then_inc(S("decay_exp"), 1)
                        act.activation(EGL, CUM48[:, 32:48], ACT.Exp).then_inc(S("decay_exp"), 1)
                    if i == 16:
                        for t in range(4):
                            act.wait_ge(S("qk_sum"), t + 1)
                            act.activation(T[:, 2 + t], ps[4 + t][:], ACT.Sqrt, bias=EPS[:, 0:1]).then_inc(
                                S("qk_root"), 1)
                for i in range(4):
                    split_hi(act, 0, B_V + i + 2)
                for t in range(TT):
                    act.wait_ge(used, B_V + 4)
                    act.activation(V[:, t], ps[4 + t][:], ACT.Copy).then_inc(S("v_evac"), 1)
                act.wait_ge(S("dw"), 2 * KDW)
                act.wait_ge(S("qk_norm"), 4)
                for j in range(2):
                    act.activation(T[:, 4 + j], DWA[:, j], ACT.Square).then_inc(S("dw_sq"), 1)
                for j in range(2):
                    act.wait_ge(S("conv_var"), j + 1)
                    act.activation(T[:, 2 + j], T[:, 2 + j], ACT.Sqrt).then_inc(S("conv_sd"), 1)
                for j in range(2):
                    act.wait_ge(S("conv_norm"), 3 + j)
                    act.activation(T[:, j], DWA[:, j], ACT.Silu, bias=prm(P_CNB + j),
                                   scale=prm(P_CNG + j)).then_inc(S("yc"), 1)
                for j in range(2):
                    act.wait_ge(S("yc"), j + 1)
                    act.activation(XH[:, 4 + j], T[:, j], ACT.Copy).then_inc(S("yc_hi"), 1)

                for h in range(H):
                    act.wait_ge(S("fox_cum"), h + 1)
                    act.activation(CUMB[:, h], ps[4 + h][:], ACT.Copy).then_inc(S("fox_cumb"), 1)

                def sb_log(h):
                    need(act, S("sb_sp"), 3 * h)
                    for i, (c0, w) in enumerate(SBW):
                        act.wait_ge(S("sb_z"), 3 * h + i + 1)
                        act.activation(T[:, i, :w], ps[i][:, :w], ACT.Abs).then_inc(S("sb_abs"), 1)
                    for i, (c0, w) in enumerate(SBW):
                        act.wait_ge(S("sb_abs"), 3 * h + i + 1)
                        act.activation(T[:, i, :w], T[:, i, :w], ACT.Exp, scale=-1.0).then_inc(S("sb_exp"), 1)
                    for i, (c0, w) in enumerate(SBW):
                        act.wait_ge(S("sb_exp"), 3 * h + i + 1)
                        act.activation(T[:, i, :w], T[:, i, :w], ACT.Ln, bias=1.0).then_inc(S("sb_ln"), 1)

                def sb_weights(h):
                    need(act, S("sb_o"), h)
                    for i, (c0, w) in enumerate(SBW):
                        act.wait_ge(S("sb_sum"), 3 * h + i + 1)
                        act.activation(SW[:, c0:c0 + w], ps[i][:, :w], ACT.Exp).then_inc(S("sb_w"), 1)

                def pair_hi(q):
                    act.wait_ge(S("sb_o"), 2 * q + 2)
                    act.activation(XH[:, 6 + q], ps[3][:], ACT.Copy).then_inc(S("yd_hi"), 1)
                    act.wait_ge(S("fox_o"), 8 * q + 8)
                    act.activation(XH[:, 2 + q], ps[7][:], ACT.Copy).then_inc(S("yb_hi"), 1)

                act.wait_ge(S("yc_lo"), 2)
                act.wait_ge(S("conv_norm"), 4)
                act.preload_act_table_set("natural_log_exp_and_others")
                for n in range(16 + 2):
                    h, s = n // 4, n % 4
                    if s == 0 and h < H:
                        sb_log(h)
                    if s == 2 and h < H:
                        sb_weights(h)
                    if n >= 2:
                        m = n - 2
                        w = (m % 4 + 1) * P
                        act.wait_ge(S("fox_t"), m + 1)
                        need(act, S("fox_o"), m - 1)
                        act.activation(PT[:, m % 2, :w], ps[6][:, :w], ACT.Copy).then_inc(S("fox_pt"), 1)
                    if n < 16:
                        w = (s + 1) * P
                        act.wait_ge(S("fox_m"), n + 1)
                        need(act, S("fox_t"), n - 2)
                        act.activation(FP[:, n % 3, :w], T[:, 3 + n % 3, :w], ACT.Exp, bias=NM[:, n:n + 1],
                                       accum_out=RS[:, n:n + 1]).then_inc(S("fox_e"), 1)
                    if n == 10:
                        pair_hi(0)
                pair_hi(1)

                for h in range(H):
                    b = 3 * (h % 2)
                    act.wait_ge(S("gdn_clip"), 2 * h + 1)
                    act.activation(T[:, b + 1], T[:, b + 1], ACT.Exp).then_inc(S("gdn_exp"), 1)
                    act.wait_ge(S("gdn_clip"), 2 * h + 2)
                    act.activation(T[:, b + 2], T[:, b + 2], ACT.Exp, scale=-1.0).then_inc(S("gdn_exp"), 1)
                for i in range(5 * H):
                    act.wait_ge(S("gdn_q"), i + 1)
                    need(act, S("gdn_pxy"), i - 3)
                    act.activation(QB[:, i % H], ps[i % 2][:], ACT.Copy).then_inc(S("gdn_qe"), 1)
                act.wait_ge(S("gdn_uw"), 1)
                for q in range(2):
                    act.activation(U[:, 8 * q:8 * q + 8, :].rearrange("p a b -> p (a b)"), ps[6 + q][:],
                                   ACT.Copy).then_inc(S("gdn_uwe"), 1)
                for q in range(2):
                    act.activation(WT[:, q], ps[q][:], ACT.Copy).then_inc(S("gdn_uwe"), 1)
                act.wait_ge(S("gdn_o"), 2)
                act.activation(OSQ[:], OT[:], ACT.Square).then_inc(S("gdn_osq"), 1)
                act.wait_ge(S("gdn_ms"), 2)
                act.activation(OS16, OS16, ACT.Sqrt).then_inc(S("gdn_rms"), 1)
                for j in range(2):
                    act.wait_ge(S("ya"), j + 1)
                    act.activation(XH[:, j], T[:, j], ACT.Copy).then_inc(S("ya_hi"), 1)

                for d in range(KT):
                    split_hi(act, 0, B_OUT + 2 + d)
                    ln_square_act(act, "b", d)
                ln_sqrt_act(act, "b")
                act.wait_ge(S("mem_landed"), 16)
                act.activation(MTH[:], MT[:], ACT.Copy).then_inc(S("mem_hi"), 1)
                for i in range(16):
                    split_hi(act, 0, B_MK + 2 + i)
                    if i < 8:
                        act.wait_ge(used, B_MK + i + 1)
                        act.activation(KM[:, i], ps[i % 4][:, :NMEM], ACT.Copy).then_inc(S("mk_evac"), 1)
                    elif i in (11, 15):
                        hh = (i - 11) // 4
                        act.wait_ge(used, B_MV + 4 * hh + 4)
                        for m in range(2):
                            act.activation(VM[:, m, 512 * hh:512 * hh + 512], ps[4 + m][:],
                                           ACT.Copy).then_inc(S("mv_evac"), 1)
                    if 2 <= i < 11:
                        ln_affine_act(act, "b", 1, i - 2)
                for i in range(KT):
                    split_hi(act, 0, B_MQ + 2 + i)
                    act.wait_ge(used, B_MQ + i + 1)
                    act.activation(MQ[:, i], ps[i % 4][:], ACT.Copy, scale=1.0 / 16).then_inc(S("mq_evac"), 1)

                def mem_out(h):
                    for c in range(2):
                        act.wait_ge(S("mem_o"), 2 * h + c + 1)
                        act.activation(XH[:, 2 * h + c], ps[4 + c][:], ACT.Copy).then_inc(S("mem_ohi"), 1)

                for n in range(16 + 2):
                    if n < 16:
                        act.wait_ge(S("mem_m"), n + 1)
                        need(act, S("mem_t"), n - 2)
                        act.activation(T[:, n % 3, :NMEM], ps[MSB[n % 3]][:, :NMEM], ACT.Exp, bias=NM[:, n:n + 1],
                                       accum_out=RS[:, n:n + 1]).then_inc(S("mem_a"), 1)
                    if n >= 2:
                        m = n - 2
                        h, t = m // 4, m % 4
                        act.wait_ge(S("mem_t"), m + 1)
                        if h >= 2 and t == 0:
                            act.wait_ge(S("mem_o"), 2 * (h - 2) + 2)
                        act.activation(MP[:, h % 2, :, t * P:(t + 1) * P],
                                       ps[2 + m % 2][:, :NMEM].rearrange("p (a b) -> p a b", a=2),
                                       ACT.Copy).then_inc(S("mem_pt"), 1)
                    if n >= 8 and n % 4 == 0:
                        mem_out((n - 8) // 4)
                mem_out(3)
                for d in range(KT):
                    split_hi(act, 0, B_MO + 2 + d)
                    ln_square_act(act, "c", d)
                ln_sqrt_act(act, "c")
                for d in range(KT + 1):
                    ln_affine_act(act, "c", 2, d)

                ffn_act(act, "d", B_UP2, B_END)
                ln_sqrt_act(act, "d")
                for d in range(KT + 1):
                    ln_affine_act(act, "d", 3, d)

            @block.vector
            def _(dve):
                ffn_dve(dve, "a", B_UP1)

                dve.memset(RAW6[:, :, 0:3], 0.0).then_inc(S("pads"), 1)
                dve.memset(GLU[:, :, 0:30], 0.0).then_inc(S("pads"), 1)
                dve.memset(ST, 0.0).then_inc(S("pads"), 1)
                gs = [0]

                def link(ins):
                    gs[0] += 1
                    ins.then_inc(S("gates_chain"), 1)
                    dve.wait_ge(S("gates_chain"), gs[0])

                dve.wait_ge(S("gates"), 1)
                dve.wait_ge(S("prm_landed"), 16)
                dve.tensor_copy(G, ps[4][:, 0:48]).then_inc(S("gates_evac"), 1)
                dve.wait_ge(S("gates_evac"), 1)
                Gv = G.rearrange("p (t c) -> p t c", c=12)
                Uv = U8.rearrange("p (g t c) -> p g t c", g=2, c=4)
                dve.tensor_tensor(Uv[:, 0], Gv[:, :, 0:4], prm(P_DT, 4).unsqueeze(1).to_broadcast([P, 4, 4]), ALU.add)
                link(dve.scalar_tensor_tensor(Uv[:, 1], Gv[:, :, 8:12], -1.0,
                                              prm(P_FB, 4).unsqueeze(1).to_broadcast([P, 4, 4]), ALU.mult,
                                              ALU.subtract))
                dve.scalar_tensor_tensor(AB, U8, -1.0, U8, ALU.mult, ALU.max).then_inc(S("gates_abs"), 1)
                dve.wait_ge(S("gates_act"), 4)
                link(dve.scalar_tensor_tensor(SPL, U8, 0.0, AB, ALU.max, ALU.add))
                link(dve.scalar_tensor_tensor(
                    LD.rearrange("p (t h) -> p t h", h=4), SPL[:, 0:16].rearrange("p (t h) -> p t h", h=4), -1.0,
                    EA.unsqueeze(1).to_broadcast([P, 4, 4]), ALU.mult, ALU.mult))
                link(dve.tensor_scalar(LF, SPL[:, 16:32], -1.0, None, ALU.mult))
                link(dve.tensor_scalar(EB, EB, 1.0, None, ALU.add))
                dve.reciprocal(BETA, EB).then_inc(S("gates_log"), 1)

                dve.wait_ge(S("pads"), 3)
                cv = S("gdn_conv")
                for t in range(6):
                    evac_wait(dve, t)
                    dve.tensor_scalar(C6[:, t], RAW6[:, t, 0:SEQ], prm(P_GCONV + 4 * t), None, ALU.mult).then_inc(cv, 1)
                    for i in range(1, KCONV):
                        dve.wait_ge(cv, 4 * t + i)
                        dve.scalar_tensor_tensor(C6[:, t], RAW6[:, t, i:i + SEQ], prm(P_GCONV + 4 * t + i), C6[:, t],
                                                 ALU.mult, ALU.add).then_inc(cv, 1)
                for j in range(2):
                    evac_wait(dve, 6 + 2 * j)
                    dve.wait_ge(used, B_IN + 8 + 2 * j)
                    dve.tensor_tensor(GLU[:, j, 30:], T[:, j], ps[(7 + 2 * j) % 4][:], ALU.mult).then_inc(
                        S(f"proj_evac{(7 + 2 * j) % 4}"), 1)
                    if j == 0:
                        dve.wait_ge(S("decays"), 1)
                        dve.tensor_copy(CUM48, ps[5][:, 0:48]).then_inc(S("decays_evac"), 1)
                        dve.wait_ge(S("decays_evac"), 1)
                        dve.tensor_tensor(KDC, CUM48[:, 16:32], CUM48[:, 0:16], ALU.subtract).then_inc(
                            S("decays_evac"), 1)
                evac_wait(dve, 7)
                evac_wait(dve, 9)
                for i in range(KDW):
                    for j in range(2):
                        src, w = GLU[:, j, i:i + SEQ], prm(P_DWW + KDW * j + i)
                        if i == 0:
                            ins = dve.tensor_scalar(DWA[:, j], src, w, prm(P_DWB + j), ALU.mult, ALU.add)
                        else:
                            dve.wait_ge(S("dw"), 2 * (i - 1) + j + 1)
                            ins = dve.scalar_tensor_tensor(DWA[:, j], src, w, DWA[:, j], ALU.mult, ALU.add)
                        ins.then_inc(S("dw"), 1)
                dve.wait_ge(S("decay_exp"), 3)
                dve.tensor_tensor(BEG, BETA, EG, ALU.mult)
                dve.tensor_scalar(EG8, EG, 0.125, None, ALU.mult).then_inc(S("coef"), 1)
                for t in range(4):
                    dve.wait_ge(S("qk_root"), t + 1)
                    dve.reciprocal(T[:, 2 + t], T[:, 2 + t]).then_inc(S("qk_inv"), 1)
                    dve.wait_ge(S("qk_inv"), t + 1)
                    dve.tensor_tensor(C6[:, t], C6[:, t], T[:, 2 + t], ALU.mult).then_inc(S("qk_norm"), 1)

                def per_head(q, coef):
                    return coef.rearrange("p (t h) -> p t h", h=4)[:, :, 2 * q:2 * q + 2].unsqueeze(3).to_broadcast(
                        [P, 4, 2, 64])

                def pair_of(ten, q):
                    return ten[:].rearrange("p (t h) d -> p t h d", h=4)[:, :, 2 * q:2 * q + 2, :]

                dve.wait_ge(S("coef"), 1)
                for q in range(2):
                    src = ps[q][:].rearrange("p (t h d) -> p t h d", t=4, h=2)
                    dve.wait_ge(S("kv_tok"), q + 1)
                    dve.tensor_tensor(pair_of(KBE, q), src, per_head(q, BEG), ALU.mult).then_inc(S("kv_scaled"), 1)
                    dve.tensor_tensor(pair_of(KD, q), src, per_head(q, KDC), ALU.mult).then_inc(S("kv_scaled"), 1)
                for q in range(2):
                    src = ps[2 + q][:].rearrange("p (t h d) -> p t h d", t=4, h=2)
                    dve.wait_ge(S("kv_tok"), 3 + q)
                    dve.tensor_tensor(pair_of(VB, q), src, per_head(q, BETA), ALU.mult).then_inc(S("kv_scaled"), 1)

                cs = S("conv_chain")
                for j in range(2):
                    dve.wait_ge(S("dw_sum"), j + 1)
                    dve.tensor_scalar(T[:, j], ps[2 * j][:], 1.0 / 64, None, ALU.mult).then_inc(cs, 1)
                    dve.wait_ge(cs, 4 * j + 1)
                    dve.tensor_tensor(T[:, 4 + j], T[:, j], T[:, j], ALU.mult).then_inc(cs, 1)
                    dve.wait_ge(cs, 4 * j + 2)
                    dve.scalar_tensor_tensor(T[:, 2 + j], ps[2 * j + 1][:], 1.0 / 64, T[:, 4 + j], ALU.mult,
                                             ALU.subtract).then_inc(cs, 1)
                    dve.wait_ge(cs, 4 * j + 3)
                    dve.tensor_scalar(T[:, 2 + j], T[:, 2 + j], 0.0, LN_EPS, ALU.max, ALU.add).then_inc(
                        S("conv_var"), 1)
                    dve.tensor_tensor(DWA[:, j], DWA[:, j], T[:, j], ALU.subtract).then_inc(cs, 1)
                for j in range(2):
                    dve.wait_ge(S("conv_sd"), j + 1)
                    dve.reciprocal(T[:, 2 + j], T[:, 2 + j]).then_inc(S("conv_norm"), 1)
                for j in range(2):
                    dve.wait_ge(S("conv_norm"), 2 + j)
                    dve.wait_ge(cs, 8)
                    dve.tensor_tensor(DWA[:, j], DWA[:, j], T[:, 2 + j], ALU.mult).then_inc(S("conv_norm"), 1)

                def sb_softplus(h):
                    need(dve, S("sb_sum"), 3 * h)
                    for i, (c0, w) in enumerate(SBW):
                        dve.wait_ge(S("sb_ln"), 3 * h + i + 1)
                        dve.scalar_tensor_tensor(SP[:, c0:c0 + w], ps[i][:, :w], 0.0, T[:, i, :w],
                                                 ALU.max, ALU.add).then_inc(S("sb_sp"), 1)

                def pair_lo(q):
                    dve.wait_ge(S("yd_hi"), q + 1)
                    dve.tensor_tensor(XL[:, 6 + q], ps[3][:], f32(XH[:, 6 + q]), ALU.subtract).then_inc(S("yd_lo"), 1)
                    dve.wait_ge(S("yb_hi"), q + 1)
                    dve.tensor_tensor(XL[:, 2 + q], ps[7][:], f32(XH[:, 2 + q]), ALU.subtract).then_inc(S("yb_lo"), 1)

                for n in range(16 + 1):
                    h, s = n // 4, n % 4
                    if s == 1:
                        sb_softplus(h)
                    if n < 16:
                        w = (s + 1) * P
                        dve.wait_ge(S("fox_s"), n + 1)
                        dve.wait_ge(S("fox_cumb"), h + 1)
                        need(dve, S("fox_e"), n - 2)
                        dve.tensor_tensor(T[:, 3 + n % 3, :w], ps[4 + n % 2][:, :w], CUMB[:, h, :w],
                                          ALU.subtract).then_inc(S("fox_a"), 1)
                        dve.wait_ge(S("fox_a"), n + 1)
                        dve.tensor_reduce(NM[:, n:n + 1], T[:, 3 + n % 3, :w], AX.X, ALU.max, negate=True).then_inc(
                            S("fox_m"), 1)
                    if n >= 1:
                        m = n - 1
                        w = (m % 4 + 1) * P
                        dve.wait_ge(S("fox_e"), m + 1)
                        dve.reciprocal(RI[:, m:m + 1], RS[:, m:m + 1]).then_inc(S("fox_r"), 1)
                        dve.wait_ge(S("fox_r"), m + 1)
                        dve.tensor_scalar(FP[:, m % 3, :w], FP[:, m % 3, :w], RI[:, m:m + 1], None,
                                          ALU.mult).then_inc(S("fox_p"), 1)
                    if n == 10:
                        pair_lo(0)
                pair_lo(1)

                def tiles(ap):
                    return ap.rearrange("p (t c) -> p t c", t=TT)

                def coef_tile(coef, h):
                    return coef.rearrange("p (t h) -> p t h", h=4)[:, :, h:h + 1].to_broadcast([P, TT, P])

                def mask(n):
                    return cst(n).unsqueeze(1).to_broadcast([P, TT, P])

                gc = S("gdn_chain")
                for h in range(H):
                    b = 3 * (h % 2)
                    dve.wait_ge(S("gdn_kk"), h + 1)
                    dve.tensor_tensor(tiles(T[:, b]), tiles(ps[b + 2][:]), coef_tile(CUM48[:, 0:16], h),
                                      ALU.subtract).then_inc(gc, 1)
                    dve.wait_ge(gc, 4 * h + 1)
                    dve.tensor_scalar(T[:, b + 1], T[:, b], 0.0, None, ALU.min).then_inc(S("gdn_clip"), 1)
                    dve.tensor_scalar(T[:, b + 2], T[:, b], 0.0, None, ALU.max).then_inc(S("gdn_clip"), 1)
                    dve.wait_ge(S("gdn_exp"), 2 * h + 1)
                    dve.tensor_tensor(tiles(T[:, b + 1]), tiles(T[:, b + 1]), mask("mdt"), ALU.mult).then_inc(gc, 1)
                    dve.wait_ge(S("gdn_exp"), 2 * h + 2)
                    dve.tensor_tensor(tiles(T[:, b + 2]), tiles(T[:, b + 2]), mask("ml"), ALU.mult).then_inc(gc, 1)
                    dve.wait_ge(gc, 4 * h + 2)
                    dve.scalar_tensor_tensor(AT[:, h], ps[b + 1][:], 0.125, T[:, b + 1], ALU.mult, ALU.mult).then_inc(
                        S("gdn_at"), 1)
                    dve.wait_ge(gc, 4 * h + 3)
                    dve.tensor_tensor(T[:, b + 2], T[:, b + 2], ps[b][:], ALU.mult).then_inc(gc, 1)
                    dve.wait_ge(gc, 4 * h + 4)
                    dve.tensor_tensor(tiles(L[:, h]), tiles(T[:, b + 2]), coef_tile(BETA, h), ALU.mult).then_inc(
                        S("gdn_l"), 1)
                for h in range(H):
                    dve.wait_ge(S("gdn_nb"), h + 1)
                    dve.wait_ge(S("gdn_t0"), h + 1)
                    dve.tensor_tensor(tiles(X[:, h]), mask("ident"), tiles(NB[:, h]), ALU.subtract)
                    dve.tensor_tensor(tiles(Y[:, h]), mask("ident"), tiles(ps[h % 2][:]), ALU.subtract).then_inc(
                        S("gdn_xy"), 1)
                for i in range(5 * H):
                    h = i % H
                    dve.wait_ge(S("gdn_pxy"), i + 1)
                    dve.wait_ge(S("gdn_xy"), i + 1)
                    if i < 4 * H:
                        dve.tensor_tensor(X[:, h], X[:, h], ps[2 + i % 2][:], ALU.subtract)
                    dve.tensor_tensor(Y[:, h], Y[:, h], ps[4 + i % 2][:], ALU.subtract).then_inc(S("gdn_xy"), 1)
                dve.wait_ge(S("gdn_uwe"), 4)
                for n in range(NC):
                    t, p0 = n // 2, slice(64 * (n % 2), 64 * (n % 2) + 64)
                    dve.wait_ge(S("gdn_pv"), n + 1)
                    for e in range(2):
                        last = dve.tensor_tensor(VN[p0, e:H:2, :], U[p0, t * H + e:t * H + H:2, :],
                                                 ps[6 * (1 - e)][p0, 0:2 * HD].rearrange("p (h d) -> p h d", h=2),
                                                 ALU.subtract)
                    last.then_inc(S("gdn_vn"), 1)
                    dve.wait_ge(S("gdn_pk"), n + 1)
                    dve.scalar_tensor_tensor(ST[:, 0], ST[:, 0], EGL[:, n:n + 1], ps[7][:, 0:HD], ALU.mult, ALU.add)
                    dve.scalar_tensor_tensor(ST[:, 1], ST[:, 1], EGL[:, 8 + n:9 + n], ps[7][:, HD:2 * HD], ALU.mult,
                                             ALU.add).then_inc(S("gdn_state"), 1)
                    dve.wait_ge(S("gdn_state"), n + 1)
                dve.wait_ge(S("gdn_oo"), 1)

                def heads16(ap, n=8):
                    return ap.unsqueeze(2).to_broadcast([P, n, HD])

                for e in range(2):
                    dve.tensor_tensor(T[:, e].rearrange("p (t a d) -> p t a d", t=TT, a=2),
                                      ps[2 + e][:].rearrange("p (t a d) -> p t a d", t=TT, a=2),
                                      EG8.rearrange("p (t h) -> p t h", h=H)[:, :, e:H:2].unsqueeze(3).to_broadcast(
                                          [P, TT, 2, HD]), ALU.mult).then_inc(S("gdn_oq"), 1)
                for tb in range(2):
                    for e in range(2):
                        dve.wait_ge(S("gdn_oq"), e + 1)
                        last = dve.tensor_tensor(
                            OT[:].rearrange("p (t h) d -> p t h d", h=H)[:, 2 * tb:2 * tb + 2, e:H:2, :],
                            T[:, e].rearrange("p (t a d) -> p t a d", t=TT, a=2)[:, 2 * tb:2 * tb + 2],
                            ps[4 + tb][:].rearrange("p (t h d) -> p t h d", t=2, h=H)[:, :, e:H:2, :], ALU.add)
                    last.then_inc(S("gdn_o"), 1)
                dve.wait_ge(S("gdn_osq"), 1)
                dve.tensor_reduce(OS16, OSQ[:], AX.X, ALU.add).then_inc(S("gdn_ms"), 1)
                dve.wait_ge(S("gdn_ms"), 1)
                dve.tensor_scalar(OS16, OS16, 1.0 / HD, RMS_EPS, ALU.mult, ALU.add).then_inc(S("gdn_ms"), 1)
                dve.wait_ge(S("gdn_rms"), 1)
                dve.reciprocal(TMP16, OS16).then_inc(S("gdn_ms"), 1)
                dve.wait_ge(S("gdn_ms"), 3)
                dve.tensor_tensor(OT[:], OT[:], heads16(TMP16, 16), ALU.mult).then_inc(S("gdn_on"), 1)
                for q in range(2):
                    dve.wait_ge(S("gdn_ot"), q + 1)
                    dve.scalar_tensor_tensor(T[:, q], ps[q][:], prm(P_GNG), ZS[:, q], ALU.mult, ALU.mult).then_inc(
                        S("ya"), 1)

                ln_gather_dve(dve, "b", ALPHA, lambda d: B_OUT + d + 1)
                ln_dve(dve, "b", LN_EPS)

                for n in range(16 + 1):
                    if n < 16:
                        dve.wait_ge(S("mem_s"), n + 1)
                        dve.tensor_reduce(NM[:, n:n + 1], ps[MSB[n % 3]][:, :NMEM], AX.X, ALU.max, negate=True).then_inc(
                            S("mem_m"), 1)
                    if n >= 1:
                        m = n - 1
                        dve.wait_ge(S("mem_a"), m + 1)
                        dve.reciprocal(RI[:, m:m + 1], RS[:, m:m + 1]).then_inc(S("mem_r"), 1)
                        dve.wait_ge(S("mem_r"), m + 1)
                        dve.tensor_scalar(T[:, m % 3, :NMEM], T[:, m % 3, :NMEM], RI[:, m:m + 1], None,
                                          ALU.mult).then_inc(S("mem_p"), 1)
                    if n >= 8 and (n - 8) % 4 == 0:
                        h = (n - 8) // 4
                        for c in range(2):
                            dve.wait_ge(S("mem_ohi"), 2 * h + c + 1)
                            dve.tensor_tensor(XL[:, 2 * h + c], ps[4 + c][:], f32(XH[:, 2 * h + c]),
                                              ALU.subtract).then_inc(S("mem_olo"), 1)
                for c in range(2):
                    dve.wait_ge(S("mem_ohi"), 7 + c)
                    dve.tensor_tensor(XL[:, 6 + c], ps[4 + c][:], f32(XH[:, 6 + c]), ALU.subtract).then_inc(
                        S("mem_olo"), 1)
                ln_gather_dve(dve, "c", ALPHA, lambda d: B_MO + d + 1)
                ln_dve(dve, "c", LN_EPS)

                ffn_dve(dve, "d", B_UP2)

        nums = sorted(s.num for s in sems.values())
        assert nums == list(range(nums[0], nums[0] + len(nums))), nums
        nc.sync.sem_clear(range(nums[0], nums[-1] + 1))
        nc.all_engine_barrier()

    stored = nc.alloc_semaphore("stored")
    with nc.Block() as block:
        @block.sync
        def _(sp):
            sp.dma_start(out, XT[:]).then_inc(stored, 16)
            sp.wait_ge(stored, 16)


def lay_out(inp):
    a = {k: np.asarray(v) for k, v in inp.items()}
    n = DEPTH

    def by_tile(w):
        return w.reshape(n, KT, P, -1, P).transpose(0, 3, 2, 1, 4).reshape(n, -1, P, BW)

    def by_k(w):
        return w.reshape(n, 4, 2, P, 512).transpose(0, 1, 3, 2, 4).reshape(n, 4, P, BW)

    def up(t):
        g, u = by_tile(a[t + "_w_gate"]), by_tile(a[t + "_w_up"])
        return np.stack([g, u], axis=2).reshape(n, 2 * FT, P, BW)

    w = a["w_in"]
    gq, gz, ga, fq, ff, cg, sq = 0, 768, 1024, 1032, 1800, 1804, 2316
    order = [gq, gq + 128, gq + 256, gq + 384, gq + 512, gq + 640,
             cg + 256, cg, cg + 384, cg + 128,
             sq, sq + 128, sq + 256, sq + 384, fq, fq + 128, fq + 256, fq + 384, gz, gz + 128]
    w_feat = by_tile(np.concatenate([w[:, :, c:c + 128] for c in order], axis=2))
    w_v = by_k(np.concatenate([w[:, :, fq + 512:fq + 768], w[:, :, sq + 512:sq + 768]], axis=2))
    kv = a["mem_w_kv"]
    wst = np.concatenate([
        up("ffn1"), w_feat, w_v, by_tile(a["w_out"]), by_tile(kv[:, :, :D]), by_k(kv[:, :, D:D + 512]),
        by_k(kv[:, :, D + 512:]), by_tile(a["mem_w_q"]), by_tile(a["mem_w_o"]), up("ffn2")], axis=1)

    def down(w):
        return w.reshape(n, 2, FT // 2, P, KT, P).transpose(0, 4, 1, 3, 2, 5).reshape(n, 16, P, DW_W)

    wdn = np.concatenate([down(a["ffn1_w_down"]), down(a["ffn2_w_down"])], axis=1)

    prm = np.zeros((n, P, NPRM), np.float32)

    def col(v):
        return v.reshape(n, -1, P).transpose(0, 2, 1)

    for i, t in enumerate(("ffn1", "mix", "mem", "ffn2")):
        prm[:, :, P_LN + 16 * i:P_LN + 16 * i + 8] = col(a[f"ln_{t}_g"])
        prm[:, :, P_LN + 16 * i + 8:P_LN + 16 * i + 16] = col(a[f"ln_{t}_b"])
    prm[:, :, P_GCONV:P_GCONV + 24] = a["gdn_conv_w"].reshape(n, KCONV, 6, P).transpose(0, 3, 2, 1).reshape(n, P, 24)
    prm[:, :, P_DWW:P_DWW + 62] = a["conf_dw_w"].reshape(n, KDW, 2, P).transpose(0, 3, 2, 1).reshape(n, P, 62)
    prm[:, :, P_DWB:P_DWB + 2] = col(a["conf_dw_b"])
    prm[:, :, P_CNG:P_CNG + 2] = col(a["conf_norm_g"])
    prm[:, :, P_CNB:P_CNB + 2] = col(a["conf_norm_b"])
    prm[:, 0:64, P_GNG] = a["gdn_norm_g"]
    prm[:, 64:128, P_GNG] = a["gdn_norm_g"]
    prm[:, :, P_DT:P_DT + 4] = a["gdn_dt_bias"][:, None, :]
    prm[:, :, P_ALOG:P_ALOG + 4] = a["gdn_a_log"][:, None, :]
    prm[:, :, P_FB:P_FB + 4] = a["fox_b_f"][:, None, :]
    wg = np.concatenate([w[:, :, ga:ga + 8], w[:, :, ff:ff + 4]], axis=2)
    prm[:, :, P_GW:] = wg.reshape(n, KT, P, 12).transpose(0, 2, 1, 3).reshape(n, P, KT * 12)

    xt = a["x"][0].T.reshape(KT, P, SEQ).transpose(1, 0, 2)
    mt = a["mem"][0].T.reshape(KT, P, NMEM).transpose(1, 0, 2)
    return {"xt": xt, "memt": mt, "wst": wst, "wdn": wdn, "prm": prm, "cst": constants()}


def kernel(**inputs):
    import concourse.bacc as bacc
    from concourse.bass_utils import run_bass_kernel_spmd

    nc = bacc.Bacc("TRN2", target_bir_lowering=False, num_devices=1)
    arrays = {k: np.ascontiguousarray(v) for k, v in lay_out(inputs).items()}
    aps = [nc.dram_tensor(k, v.shape, F32, kind="ExternalInput").ap() for k, v in arrays.items()]
    out = nc.dram_tensor("out", (P, KT, SEQ), F32, kind="ExternalOutput").ap()
    build_program(nc, *aps, out)
    r = run_bass_kernel_spmd(nc, [arrays], core_ids=[0])
    o = r.results[0]["out"]
    return np.ascontiguousarray(o.transpose(1, 0, 2).reshape(D, SEQ).T[None])
```
